# Optimizing a Trainium2 kernel written in Bass

```python
import math
import jax, jax.numpy as jnp
from jax import lax
import numpy as np

D_MODEL = 1024
BATCH = 1
SEQ = 512
DEPTH = 2

CTX_LEN = 256
GRID_W = 64
N_MOD = 9
D_FF = 2816

POOL_WINDOWS = (2, 4, 8, 16)
POOL_GROUP = 64
POOL_WIDTH = POOL_GROUP * len(POOL_WINDOWS)
MLA_HEADS = 4
MLA_NOPE = 64
MLA_ROPE = 32
MLA_V = 64
MLA_Q_RANK = 384
MLA_KV_RANK = 256
MLA_WIDTH = MLA_HEADS * MLA_V
DIFF_HEADS = 4
DIFF_DIM = 64
DIFF_V = 2 * DIFF_DIM
DIFF_WIDTH = DIFF_HEADS * DIFF_V
MIX_WIDTH = POOL_WIDTH + MLA_WIDTH + DIFF_WIDTH
IN_POOL = POOL_WIDTH
IN_MLA = MLA_Q_RANK + MLA_KV_RANK + MLA_ROPE
IN_DIFF = 3 * DIFF_HEADS * 2 * DIFF_DIM
IN_WIDTH = IN_POOL + IN_MLA + IN_DIFF
ROPE_BASE = 10000.0
Q_BLOCK = 128
EPS = 1e-6

kernel_name = "hymba_pool_mla_diff_macaron"

F32 = jnp.float32

def _rmsnorm(x, g):
    xf = x.astype(F32)
    y = xf * lax.rsqrt(jnp.mean(xf * xf, axis=-1, keepdims=True) + EPS)
    return (y * g.astype(F32)).astype(x.dtype)

def _modulate(n, shift, scale):
    return n * (1.0 + scale) + shift

def _swiglu(x, w1, w3, w2):
    return (jax.nn.silu(x @ w1) * (x @ w3)) @ w2

def _axial_rope(n_tok, rot_dim):
    t = jnp.arange(n_tok)
    row = (t // GRID_W).astype(F32)
    col = (t % GRID_W).astype(F32)
    n_axis = rot_dim // 4
    inv = ROPE_BASE ** (-jnp.arange(n_axis, dtype=F32) / n_axis)
    ang = jnp.concatenate([row[:, None] * inv, col[:, None] * inv], axis=-1)
    return jnp.cos(ang), jnp.sin(ang)

def _rope(x, cos, sin):
    h = x.shape[-1] // 2
    x1 = x[..., :h].astype(F32)
    x2 = x[..., h:].astype(F32)
    c = cos[None, :, None, :]
    s = sin[None, :, None, :]
    return jnp.concatenate([x1 * c - x2 * s, x1 * s + x2 * c], axis=-1).astype(x.dtype)

def _window_mean(u, k, axis):
    n = u.shape[axis]
    lo = k // 2
    hi = k - 1 - lo
    csum = jnp.cumsum(u.astype(F32), axis=axis)
    pad = [(0, 0)] * u.ndim
    pad[axis] = (1, 0)
    pref = jnp.pad(csum, pad)
    idx = jnp.arange(n)
    start = jnp.clip(idx - lo, 0, n)
    end = jnp.clip(idx + hi + 1, 0, n)
    tot = jnp.take(pref, end, axis=axis) - jnp.take(pref, start, axis=axis)
    cnt_shape = [1] * u.ndim
    cnt_shape[axis] = n
    cnt = (end - start).astype(F32).reshape(cnt_shape)
    return (tot / cnt).astype(u.dtype)

def _pool_mixer(u, pool_w, pool_scale, rows):
    b, n, _ = u.shape
    outs = []
    for g, k in enumerate(POOL_WINDOWS):
        ug = u[..., g * POOL_GROUP:(g + 1) * POOL_GROUP]
        if rows is None:
            m = _window_mean(ug, k, 1)
        else:
            ug2 = ug.reshape(b, rows, GRID_W, POOL_GROUP)
            m = _window_mean(_window_mean(ug2, k, 1), k, 2).reshape(b, n, POOL_GROUP)
        outs.append((m - ug) @ pool_w[g])
    return jnp.concatenate(outs, axis=-1) * pool_scale

def _mla_qkv(u, q_norm, w_uq, kv_norm, w_ukv, rope):
    b, n, _ = u.shape
    c_q = _rmsnorm(u[..., :MLA_Q_RANK], q_norm)
    c_kv = _rmsnorm(u[..., MLA_Q_RANK:MLA_Q_RANK + MLA_KV_RANK], kv_norm)
    k_rope = u[..., MLA_Q_RANK + MLA_KV_RANK:][:, :, None, :]
    q = (c_q @ w_uq).reshape(b, n, MLA_HEADS, MLA_NOPE + MLA_ROPE)
    kv = (c_kv @ w_ukv).reshape(b, n, MLA_HEADS, MLA_NOPE + MLA_V)
    q_nope, q_rope = q[..., :MLA_NOPE], q[..., MLA_NOPE:]
    if rope is not None:
        q_rope = _rope(q_rope, *rope)
        k_rope = _rope(k_rope, *rope)
    q = jnp.concatenate([q_nope, q_rope], axis=-1)
    k = jnp.concatenate([kv[..., :MLA_NOPE], jnp.broadcast_to(k_rope, (b, n, MLA_HEADS, MLA_ROPE))], axis=-1)
    v = kv[..., MLA_NOPE:]
    return q, k, v

def _diff_qkv(u, rope):
    b, n, _ = u.shape
    hq = DIFF_HEADS * 2 * DIFF_DIM
    q = u[..., :hq].reshape(b, n, 2 * DIFF_HEADS, DIFF_DIM)
    k = u[..., hq:2 * hq].reshape(b, n, 2 * DIFF_HEADS, DIFF_DIM)
    v = u[..., 2 * hq:].reshape(b, n, DIFF_HEADS, DIFF_V)
    if rope is not None:
        q = _rope(q, *rope)
        k = _rope(k, *rope)
    return q[:, :, 0::2], q[:, :, 1::2], k[:, :, 0::2], k[:, :, 1::2], v

def _sdpa(q, k, v, scale):
    s = jnp.einsum('bqhd,bkhd->bhqk', q, k).astype(F32) * scale
    p = jax.nn.softmax(s, axis=-1).astype(v.dtype)
    return jnp.einsum('bhqk,bkhd->bqhd', p, v)

def _diff_sdpa(q1, q2, k1, k2, v, scale, lam):
    p1 = jax.nn.softmax(jnp.einsum('bqhd,bkhd->bhqk', q1, k1).astype(F32) * scale, axis=-1)
    p2 = jax.nn.softmax(jnp.einsum('bqhd,bkhd->bhqk', q2, k2).astype(F32) * scale, axis=-1)
    return jnp.einsum('bhqk,bkhd->bqhd', (p1 - lam * p2).astype(v.dtype), v)

def _by_query_blocks(fn, qs):
    b, s = qs[0].shape[:2]
    nb = s // Q_BLOCK
    blocks = tuple(q.reshape(b, nb, Q_BLOCK, *q.shape[2:]).swapaxes(0, 1) for q in qs)
    out = lax.map(lambda qb: fn(*qb), blocks)
    return out.swapaxes(0, 1).reshape(b, s, *out.shape[3:])

def _diff_out(o, subln, lam_init):
    o = _rmsnorm(o, subln) * (1.0 - lam_init)
    return o.reshape(o.shape[0], o.shape[1], DIFF_WIDTH)

def _token_mixing(n_lat, n_ctx, w_in, w_out, pool_w, pool_scale, mla_q_norm, mla_w_uq, mla_kv_norm,
                  mla_w_ukv, diff_lambda, diff_subln, lam_init, rope_mla, rope_diff, rows, with_ctx):
    b, s, _ = n_lat.shape
    p_lat = n_lat @ w_in
    p_ctx = n_ctx @ w_in
    s1, s2 = IN_POOL, IN_POOL + IN_MLA
    a_lat = _pool_mixer(p_lat[..., :s1], pool_w, pool_scale, rows)
    qb, kb, vb = _mla_qkv(p_lat[..., s1:s2], mla_q_norm, mla_w_uq, mla_kv_norm, mla_w_ukv, rope_mla)
    qbc, kbc, vbc = _mla_qkv(p_ctx[..., s1:s2], mla_q_norm, mla_w_uq, mla_kv_norm, mla_w_ukv, None)
    kb_all = jnp.concatenate([kbc, kb], axis=1)
    vb_all = jnp.concatenate([vbc, vb], axis=1)
    scale_b = (MLA_NOPE + MLA_ROPE) ** -0.5
    b_lat = _by_query_blocks(lambda q: _sdpa(q, kb_all, vb_all, scale_b), (qb,))
    lq1, lk1, lq2, lk2 = diff_lambda.astype(F32)
    lam = jnp.exp(jnp.sum(lq1 * lk1)) - jnp.exp(jnp.sum(lq2 * lk2)) + lam_init
    q1, q2, k1, k2, vc = _diff_qkv(p_lat[..., s2:], rope_diff)
    q1c, q2c, k1c, k2c, vcc = _diff_qkv(p_ctx[..., s2:], None)
    k1_all = jnp.concatenate([k1c, k1], axis=1)
    k2_all = jnp.concatenate([k2c, k2], axis=1)
    vc_all = jnp.concatenate([vcc, vc], axis=1)
    scale_c = DIFF_DIM ** -0.5
    c_lat = _by_query_blocks(lambda a1, a2: _diff_sdpa(a1, a2, k1_all, k2_all, vc_all, scale_c, lam), (q1, q2))
    y_lat = jnp.concatenate([a_lat, b_lat.reshape(b, s, MLA_WIDTH), _diff_out(c_lat, diff_subln, lam_init)],
                            axis=-1) @ w_out
    if not with_ctx:
        return y_lat, None
    bc, lc, _ = n_ctx.shape
    a_ctx = _pool_mixer(p_ctx[..., :s1], pool_w, pool_scale, None)
    b_ctx = _sdpa(qbc, kbc, vbc, scale_b).reshape(bc, lc, MLA_WIDTH)
    c_ctx = _diff_out(_diff_sdpa(q1c, q2c, k1c, k2c, vcc, scale_c, lam), diff_subln, lam_init)
    y_ctx = jnp.concatenate([a_ctx, b_ctx, c_ctx], axis=-1) @ w_out
    return y_lat, y_ctx

def setup_inputs(seed: int = 0) -> dict:
    key = jax.random.key(seed)
    ks = iter(jax.random.split(key, 32))

    def nrm(shape, scale):
        return jax.random.normal(next(ks), shape, F32) * scale

    def gain(shape):
        return 1.0 + nrm(shape, 0.02)

    L = DEPTH
    return {
        "x": nrm((BATCH, SEQ, D_MODEL), 1.0),
        "c": nrm((BATCH, D_MODEL), 1.0),
        "ctx": nrm((BATCH, CTX_LEN, D_MODEL), 1.0),
        "c_ctx": nrm((D_MODEL,), 1.0),
        "w_mod": nrm((L, D_MODEL, N_MOD * D_MODEL), 0.5 * D_MODEL ** -0.5),
        "b_mod": nrm((L, N_MOD * D_MODEL), 0.01),
        "ffn1_norm": gain((L, D_MODEL)),
        "ffn1_w1": nrm((L, D_MODEL, D_FF), D_MODEL ** -0.5),
        "ffn1_w3": nrm((L, D_MODEL, D_FF), D_MODEL ** -0.5),
        "ffn1_w2": nrm((L, D_FF, D_MODEL), D_FF ** -0.5),
        "mix_norm": gain((L, D_MODEL)),
        "w_in": nrm((L, D_MODEL, IN_WIDTH), D_MODEL ** -0.5),
        "w_out": nrm((L, MIX_WIDTH, D_MODEL), MIX_WIDTH ** -0.5),
        "pool_w": nrm((L, len(POOL_WINDOWS), POOL_GROUP, POOL_GROUP), POOL_GROUP ** -0.5),
        "pool_scale": 1.0 + nrm((L, POOL_WIDTH), 0.1),
        "mla_q_norm": gain((L, MLA_Q_RANK)),
        "mla_w_uq": nrm((L, MLA_Q_RANK, MLA_HEADS * (MLA_NOPE + MLA_ROPE)), MLA_Q_RANK ** -0.5),
        "mla_kv_norm": gain((L, MLA_KV_RANK)),
        "mla_w_ukv": nrm((L, MLA_KV_RANK, MLA_HEADS * (MLA_NOPE + MLA_V)), MLA_KV_RANK ** -0.5),
        "diff_lambda": nrm((L, 4, DIFF_DIM), 0.1),
        "diff_subln": gain((L, DIFF_V)),
        "ffn2_norm": gain((L, D_MODEL)),
        "ffn2_w1": nrm((L, D_MODEL, D_FF), D_MODEL ** -0.5),
        "ffn2_w3": nrm((L, D_MODEL, D_FF), D_MODEL ** -0.5),
        "ffn2_w2": nrm((L, D_FF, D_MODEL), D_FF ** -0.5),
        "final_norm": gain((D_MODEL,)),
    }

def reference(x, c, ctx, c_ctx, w_mod, b_mod, ffn1_norm, ffn1_w1, ffn1_w3, ffn1_w2, mix_norm, w_in, w_out,
              pool_w, pool_scale, mla_q_norm, mla_w_uq, mla_kv_norm, mla_w_ukv, diff_lambda, diff_subln,
              ffn2_norm, ffn2_w1, ffn2_w3, ffn2_w2, final_norm):
    b, seq, d = x.shape
    rows = seq // GRID_W
    rope_mla = _axial_rope(seq, MLA_ROPE)
    rope_diff = _axial_rope(seq, DIFF_DIM)
    sc = jax.nn.silu(c)
    scc = jax.nn.silu(c_ctx)
    h, hc = x, ctx
    for i in range(DEPTH):
        last = i == DEPTH - 1
        m = jnp.split((sc @ w_mod[i] + b_mod[i])[:, None, :], N_MOD, axis=-1)
        mc = jnp.split((scc @ w_mod[i] + b_mod[i])[None, None, :], N_MOD, axis=-1)
        h = h + 0.5 * m[2] * _swiglu(_modulate(_rmsnorm(h, ffn1_norm[i]), m[0], m[1]),
                                     ffn1_w1[i], ffn1_w3[i], ffn1_w2[i])
        hc = hc + 0.5 * mc[2] * _swiglu(_modulate(_rmsnorm(hc, ffn1_norm[i]), mc[0], mc[1]),
                                        ffn1_w1[i], ffn1_w3[i], ffn1_w2[i])
        lam_init = 0.8 - 0.6 * math.exp(-0.3 * i)
        n_lat = _modulate(_rmsnorm(h, mix_norm[i]), m[3], m[4])
        n_ctx = _modulate(_rmsnorm(hc, mix_norm[i]), mc[3], mc[4])
        y, yc = _token_mixing(n_lat, n_ctx, w_in[i], w_out[i], pool_w[i], pool_scale[i], mla_q_norm[i],
                              mla_w_uq[i], mla_kv_norm[i], mla_w_ukv[i], diff_lambda[i], diff_subln[i],
                              lam_init, rope_mla, rope_diff, rows, not last)
        h = h + m[5] * y
        h = h + 0.5 * m[8] * _swiglu(_modulate(_rmsnorm(h, ffn2_norm[i]), m[6], m[7]),
                                     ffn2_w1[i], ffn2_w3[i], ffn2_w2[i])
        if not last:
            hc = hc + mc[5] * yc
            hc = hc + 0.5 * mc[8] * _swiglu(_modulate(_rmsnorm(hc, ffn2_norm[i]), mc[6], mc[7]),
                                            ffn2_w1[i], ffn2_w3[i], ffn2_w2[i])
    return _rmsnorm(h, final_norm)


_drawn_inputs = setup_inputs


def setup_inputs(seed=0):
    import zlib

    import numpy as np

    out = dict(_drawn_inputs(seed))
    spreads = {}
    factors = {'b_mod': 3.601,
     'ffn1_norm': 8.0,
     'mix_norm': 8.0,
     'pool_scale': 2.881,
     'mla_q_norm': 8.0,
     'mla_w_uq': 3.284,
     'mla_kv_norm': 8.0,
     'diff_lambda': 8.0,
     'diff_subln': 42.873,
     'ffn2_norm': 8.0,
     'final_norm': 7.956}
    for name, (base, spread) in spreads.items():
        noise = np.random.default_rng([zlib.crc32(name.encode()), seed]).standard_normal(out[name].shape)
        drawn = base * np.exp(spread * noise) if base else spread * noise
        out[name] = __import__('jax').numpy.asarray(drawn.astype(out[name].dtype))
    for name, factor in factors.items():
        out[name] = (out[name] * factor).astype(out[name].dtype)
    return out
```

```python
import math
from contextlib import ExitStack

import numpy as np
import concourse.bass as bass
from concourse import mybir

P = 128
D, SEQ, CTX, DEPTH = 1024, 512, 256, 2
TOK = SEQ + CTX
GRID_W = 64
ROWS = SEQ // GRID_W
N_MOD = 9
D_FF = 2816
KD = D // P
FT = D_FF // P
GROUPS = 2
FG = FT // GROUPS
HEADS = 4
NOPE, ROPE, MV = 64, 32, 64
QR, KVR = 384, 256
DDIM = 64
IN_POOL = 256
IN_MLA = QR + KVR + ROPE
EPS = 1e-6
ROPE_BASE = 10000.0
WINDOWS = (2, 4, 8, 16)
PAD = 8
UNITS_MOD = N_MOD * KD
PRO_UNITS = 2 * KD
MOD_T = 2
MOD_W = MOD_T * P
T_POOL, T_Q, T_KV, T_KR, T_DQ, T_DK, T_DV, T_IN = 0, 2, 5, 7, 8, 12, 16, 20
M_POOL, M_MLA, M_DIFF = 0, 2, 4
SC_MLA = (NOPE + ROPE) ** -0.5
SC_DIFF = DDIM ** -0.5
LAM_INIT = [0.8 - 0.6 * math.exp(-0.3 * i) for i in range(DEPTH)]
G_FFN1, G_MIX, G_FFN2, G_POOL, G_QN, G_KVN, G_SUB, G_LAYER = 0, 8, 16, 24, 26, 29, 31, 32
G_FINAL = DEPTH * G_LAYER
G_ROWS = G_FINAL + KD

F32 = mybir.dt.float32
F32R = mybir.dt.float32r
ALU = mybir.AluOpType
ACT = mybir.ActivationFunctionType
AX = mybir.AxisListType


def plan_sweeps():
    sweeps, base = [], 0

    def add(layer, what, n, kt, ctx, arg=0):
        nonlocal base
        sweeps.append(dict(layer=layer, what=what, n=n, kt=kt, ctx=ctx, arg=arg, base=base))
        base += n

    for i in range(DEPTH):
        more = i < DEPTH - 1
        for ffn in ("ffn1", "ffn2"):
            both = (ffn == "ffn1" or more,) * 2
            for g in range(GROUPS):
                add(i, ffn + "_up", FG, KD, both, g)
                add(i, ffn + "_down", KD // 2, FG, both, g)
            if ffn == "ffn1":
                add(i, "in", 2, KD, (more, more), 0)
                add(i, "in", 1, KD, (more, True), 4)
                add(i, "in", 1, KD, (True, True), 6)
                add(i, "in", 2, KD, (more, more), 8)
                add(i, "in", 4, KD, (True, True), 12)
                add(i, "out", KD // 2, KD, (more, more))
    return sweeps


def mod_tile(w):
    if w["layer"] == 0 and w["what"].startswith("ffn"):
        return PRO_UNITS + MOD_T * sum(v["n"] for v in plan_sweeps() if v["base"] < w["base"] and v["layer"] == 0
                                       and v["what"].startswith("ffn"))
    if w["layer"] == 1 and w["what"] == "ffn1_down" and w["arg"] == 0:
        return DEPTH * UNITS_MOD - MOD_T * w["n"]
    return None


def plan_groups(more):
    spans = [(0, SEQ, 0, TOK)] + ([(SEQ, CTX, SEQ, CTX)] if more else [])
    diff = [("diff", j, *s) for j in range(HEADS) for s in spans]
    mla = [("mla", 2 * m + e, *s) for m in range(HEADS // 2) for s in spans for e in range(2)]
    return diff, mla


def halves(n):
    return [(a, min(512, n - a)) for a in range(0, n, 512)]


TASKS = ([("v", a, "ad"[a % 2]) for a in range(6)] + [("rope", a, "d") for a in range(T_DQ, T_DV)]
         + [("rope", T_KR, "d")] + [("vm", a, "a") for a in range(3)] + [("kn", a, "a") for a in range(2)]
         + [("uq", a, "a") for a in range(3)] + [("rope", T_Q + 2, "d")])


def read_out(who, count):
    return sum(1 for task in TASKS[:count] if task[2] == who)


N_ACT, N_DVE = read_out("a", len(TASKS)), read_out("d", len(TASKS))
GROUPS_OF = [sum(plan_groups(i < DEPTH - 1), []) for i in range(DEPTH)]
N_DIFF = [len(plan_groups(i < DEPTH - 1)[0]) for i in range(DEPTH)]
MIX_OF = [n + n // 2 + 2 for n in N_DIFF]


def step_buf(L, n):
    return 2 * (n % 2) if n < sum(g[3] // P for g in GROUPS_OF[L][:N_DIFF[L]]) else n % 4


def steps_of(L):
    return [(g, gi, b) for gi, g in enumerate(GROUPS_OF[L]) for b in range(g[3] // P)]


N_SMALL = 4 + 7 * DEPTH


def build(nc, t, out):
    SWEEPS = plan_sweeps()
    with ExitStack() as stack:
        def sb(name, cols, dt=F32, parts=P):
            return stack.enter_context(nc.sbuf_tensor(name, [parts, cols], dt))

        def sem(name):
            return stack.enter_context(nc.semaphore(name))

        def overlay(*specs):
            with ExitStack() as s:
                return [s.enter_context(nc.sbuf_tensor(n, [P, c], dt)) for n, c, dt in specs]

        x = sb("x", KD * TOK)
        raw_w = [sb(f"raw_w{s}", FG * P) for s in range(2)]
        hi_w = [sb(f"hi_w{s}", FG * P, F32R) for s in range(2)]
        lo_w = [sb(f"lo_w{s}", FG * P, F32R) for s in range(2)]
        ident = sb("ident", P)
        perm_d = sb("perm_d", P)
        perm_m = sb("perm_m", P)
        ones = sb("ones", P)
        mod = sb("mod", DEPTH * UNITS_MOD * 2)
        b_mod = sb("b_mod", DEPTH * UNITS_MOD)
        gains = sb("gains", G_ROWS)
        silu_c = sb("silu_c", KD * 2)
        scale_a = sb("scale_a", KD * 2)
        gate = sb("gate", KD * 2)
        neg_lam = sb("neg_lam", DEPTH)
        lam_sum = sb("lam_sum", 2 * DEPTH)
        lam_exp = sb("lam_exp", 2 * DEPTH)
        sub_gain = sb("sub_gain", DEPTH)
        eps_col = sb("eps_col", 1)
        neg_max = sb("neg_max", 8)
        max_bias = sb("max_bias", 8)
        exp_sum = sb("exp_sum", 8)
        inv_sum = sb("inv_sum", 8)
        cos_d = sb("cos_d", SEQ)
        sin_d = sb("sin_d", SEQ)
        rstd = sb("rstd", TOK)
        buf = [sb(f"buf{i}", TOK) for i in range(4)]
        act_buf, hid_buf, sq = buf[0], buf[1], buf[2:4]
        mod_w, mod_acc = overlay(("mod_w", KD * MOD_W, F32), ("mod_acc", 2 * MOD_W, F32))
        v_tok = sb("v_tok", (TOK // P) * 512)
        pro_w1, mod_rows = overlay(("pro_w1", KD * D, F32), ("mod_rows", 2 * D, F32))
        _, wq_n, wq_r, _, pool_inv, cos_m, sin_m, _, pool_w, _, wk_n, wk_v, pool_c, pool_a, pool_b = overlay(
            ("under_pool_hi", 2 * TOK, F32), ("wq_n", 3 * 256, F32), ("wq_r", 3 * P, F32),
            ("under_mla_hi", 2 * TOK - 9 * P, F32), ("pool_inv", 2 * TOK, F32), ("cos_m", SEQ, F32),
            ("sin_m", SEQ, F32), ("under_pool_lo", 2 * TOK - 2 * SEQ + TOK, F32), ("pool_w_sb", 2 * P, F32),
            ("rest_pool_lo", TOK - 2 * P, F32), ("wk_n", 512, F32), ("wk_v", 512, F32), ("pool_c", SEQ, F32),
            ("pool_a", 2 * TOK, F32), ("pool_b", 2 * TOK, F32))
        n_hi = sb("n_hi", KD * TOK, F32R)
        n_lo = sb("n_lo", KD * TOK, F32R)
        proj, v_mla = overlay(("proj", T_IN * TOK, F32), ("v_mla", (TOK // P) * 256, F32))
        x_tok, pro_w2, c_rows, rows, lam_row = overlay(("x_tok", (TOK // P) * D, F32), ("pro_w2", KD * D, F32),
                                               ("c_rows", P, F32),
                                               ("rows", 3 * P, F32), ("lam_row", DEPTH * 4 * DDIM, F32))
        lam_prod = sq[0]
        h_hi = sb("h_hi", FG * TOK, F32R)
        h_lo = sb("h_lo", FG * TOK, F32R)
        p_t = proj[:, T_DV * TOK:T_DV * TOK + 6 * 512]

        pair = [stack.enter_context(nc.psum_tensor(f"pair{i}", [P, 1024], F32)) for i in range(4)]

        raw_full = [sem(f"raw_full{s}") for s in range(2)]
        hi_ready = [sem(f"hi_ready{s}") for s in range(2)]
        lo_ready = [sem(f"lo_ready{s}") for s in range(2)]
        unit_done = [sem(f"unit_done{s}") for s in range(2)]
        pair_free = [sem(f"pair_free{s}") for s in range(2)]
        krope_full = sem("krope_full")
        c_full = sem("c_full")
        c_done = sem("c_done")
        small_full = sem("small_full")
        x_full = sem("x_full")
        pro_full = [sem("pro_full0"), sem("pro_full1")]
        cols_done = sem("cols_done")
        ones_ready = sem("ones_ready")
        cols_out = sem("cols_out")
        mrow_done = sem("mrow_done")
        mrow_out = [sem("mrow_out_act"), sem("mrow_out_dve")]
        tables_full = sem("tables_full")
        silu_ready = sem("silu_ready")
        xt_done = sem("xt_done")
        xt_out = [sem("xt_out_act"), sem("xt_out_dve")]
        lam_ready = sem("lam_ready")
        mod_full = sem("mod_full")
        mod_sum = sem("mod_sum")
        mod_done = sem("mod_done")
        mod_out = sem("mod_out")
        sq_ready = sem("sq_ready")
        sq_used = sem("sq_used")
        log_ready = sem("log_ready")
        std_ready = sem("std_ready")
        applied = sem("applied")
        t_ready = sem("t_ready")
        nhi_ready = sem("nhi_ready")
        n_ready = sem("n_ready")
        hhi_ready = sem("hhi_ready")
        h_ready = sem("h_ready")
        mixw_full = sem("mixw_full")
        poolw_zero = sem("poolw_zero")
        poolw_full = sem("poolw_full")
        counts_full = sem("counts_full")
        task_done = sem("task_done")
        out_act = sem("out_act")
        out_dve = sem("out_dve")
        pool_ready = sem("pool_ready")
        pool_chain = sem("pool_chain")
        s_ready = [sem("s_ready0"), sem("s_ready1")]
        max_ready = sem("max_ready")
        exp_done = [sem("exp_done0"), sem("exp_done1")]
        p_ready = sem("p_ready")
        t_done = sem("t_done")
        pt_ready = sem("pt_ready")
        pv_done = sem("pv_done")
        o_act = sem("o_act")
        otmp_ready = sem("otmp_ready")
        mhi_ready = sem("mhi_ready")
        mix_ready = sem("mix_ready")
        poolmm_done = sem("poolmm_done")
        fin_done = sem("fin_done")
        fin_out = sem("fin_out")
        stored = sem("stored")
        dve_chain = sem("dve_chain")

        def cols(w, i, s):
            L, what = w["layer"], w["what"]
            if what.endswith("_up"):
                src = t[what[:4] + ("_w1", "_w3")[s]][L]
                c0 = (w["arg"] * FG + i) * P
            elif what.endswith("_down"):
                src = t[what[:4] + "_w2"][L][w["arg"] * FG * P:(w["arg"] + 1) * FG * P, :]
                c0 = (2 * i + s) * P
            elif what == "in":
                src = t["w_in"][L]
                c0 = (w["arg"] + 2 * i + s) * P - (P - ROPE if w["arg"] >= T_DQ else 0)
            else:
                src, c0 = t["w_out"][L], (2 * i + s) * P
            return src.rearrange("(k p) c -> p k c", p=P)[:, :, bass.ds(c0, P)]

        def norm_width(w):
            return TOK if w["what"] == "in" else width(w, 1)

        def is_krope(w, s):
            return w["what"] == "in" and w["arg"] == 6 and s == 1

        def width(w, s):
            return TOK if w["ctx"][s] else SEQ

        def tile(tensor, k, n=TOK, at=0):
            return tensor[:, bass.ds(k * TOK + at, n)]

        def mod_col(L, chunk):
            return (L * UNITS_MOD + chunk * KD) * 2

        block = stack.enter_context(nc.Block())

        @block.sync
        def _(sp):
            def small(dst, src):
                sp.dma_start(dst, src).then_inc(small_full, 16)

            def as_rows(v):
                return v.rearrange("(r c) -> r c", c=P)

            sp.dma_start(c_rows[0:KD, :], as_rows(t["c"][0])).then_inc(c_full, 16)
            sp.dma_start(c_rows[KD:2 * KD, :], as_rows(t["c_ctx"])).then_inc(c_full, 16)
            sp.dma_start(ident[:, :], t["k_ident"]).then_inc(c_full, 16)
            for a in range(TOK // P):
                src = t["x"][0][a * P:(a + 1) * P, :] if a < SEQ // P else t["ctx"][0][a * P - SEQ:(a + 1) * P - SEQ, :]
                sp.dma_start(x_tok[:, a * D:(a + 1) * D], src).then_inc(x_full, 16)
            for L in range(DEPTH):
                small(rows[0:UNITS_MOD, L * P:(L + 1) * P], as_rows(t["b_mod"][L]))
                for name, col in (("ffn1_norm", G_FFN1), ("mix_norm", G_MIX), ("ffn2_norm", G_FFN2),
                                  ("pool_scale", G_POOL), ("mla_q_norm", G_QN), ("mla_kv_norm", G_KVN),
                                  ("diff_subln", G_SUB)):
                    v = as_rows(t[name][L])
                    r0 = L * G_LAYER + col
                    small(rows[r0:r0 + v.shape[0], 2 * P:3 * P], v)
            small(rows[G_FINAL:G_ROWS, 2 * P:3 * P], as_rows(t["final_norm"]))
            small(lam_row[0:1, :], t["diff_lambda"].rearrange("l a d -> (l a d)").rearrange("(o n) -> o n", o=1))
            wm = t["w_mod"][0].rearrange("(k p) c -> p k c", p=P)
            for m, dst in enumerate((pro_w1, pro_w2)):
                sp.dma_start(dst[:, :].rearrange("p (k c) -> p k c", k=KD), wm[:, :, m * D:(m + 1) * D])\
                  .then_inc(pro_full[m], 16)

            def load_unit(w, i, s, first):
                if not (first and w["base"] == 0):
                    sp.wait_ge(lo_ready[s], w["base"] + i)
                dst = raw_w[s][:, 0:w["kt"] * P].rearrange("p (k c) -> p k c", c=P)
                if is_krope(w, s):
                    src = t["w_in"][w["layer"]].rearrange("(k p) c -> p k c", p=P)[:, :, T_KR * P:T_KR * P + ROPE]
                    for r in range(HEADS):
                        sp.dma_start(dst[:, :, r * ROPE:(r + 1) * ROPE], src)\
                          .then_inc(krope_full if r else raw_full[s], 16)
                else:
                    sp.dma_start(dst, cols(w, i, s)).then_inc(raw_full[s], 16)

            def load_mod(w, i, before, L):
                if w["layer"] == 0 and w["what"] == "ffn2_up" and w["arg"] == 0 and isinstance(i, int):
                    sp.wait_ge(pv_done, len(GROUPS_OF[0]))
                if not (isinstance(before, int) and before == 0):
                    sp.wait_ge(mod_sum, 2 * KD * before)
                src = t["w_mod"][L].rearrange("(k p) c -> p k c", p=P)
                sp.dma_start(mod_w[:, :].rearrange("p (k c) -> p k c", k=KD),
                             src[:, :, bass.ds((mod_tile(w) - L * UNITS_MOD + MOD_T * i) * P, MOD_W)]).then_inc(mod_full, 16)

            batches = 0
            for q, w in enumerate(SWEEPS):
                u0 = mod_tile(w)
                if w["what"] != "out":
                    load_unit(w, 0, 0, True)
                    load_unit(w, 0, 1, True)
                if u0 is not None:
                    load_mod(w, 0, batches, 0 if u0 < UNITS_MOD else 1)
                cut = (UNITS_MOD - u0) // MOD_T if u0 is not None and u0 < UNITS_MOD < u0 + MOD_T * w["n"] else w["n"]
                for a, b in ((1, cut), (cut, w["n"])):
                    if a < b:
                        with sp.Fori(a, b) as i:
                            load_unit(w, i, 0, False)
                            load_unit(w, i, 1, False)
                            if u0 is not None:
                                load_mod(w, i, batches + i, int(u0 + MOD_T * a >= UNITS_MOD))
                if q == 0:
                    for dst, name in ((perm_d, "k_perm_d"), (perm_m, "k_perm_m"), (cos_d, "k_cos_d"), (sin_d, "k_sin_d")):
                        sp.dma_start(dst[:, :], t[name]).then_inc(tables_full, 16)
                if u0 is not None:
                    batches += w["n"]
                if w["what"] == "in" and w["arg"] == 12:
                    L = w["layer"]
                    load_unit(SWEEPS[q + 1], 0, 0, True)
                    load_unit(SWEEPS[q + 1], 0, 1, True)
                    for s in range(2):
                        sp.wait_ge(unit_done[s], w["base"] + w["n"])
                    uq = t["mla_w_uq"][L].rearrange("(k p) (h c) -> p k h c", p=P, h=HEADS)
                    ukv = t["mla_w_ukv"][L].rearrange("(k p) (h c) -> p k h c", p=P, h=HEADS)
                    for k in range(QR // P):
                        sp.dma_start(wq_n[:, k * 256:(k + 1) * 256].rearrange("p (h c) -> p h c", h=HEADS),
                                     uq[:, k, :, 0:NOPE]).then_inc(mixw_full, 16)
                        sp.dma_start(wq_r[:, k * P:(k + 1) * P].rearrange("p (h c) -> p h c", h=HEADS),
                                     uq[:, k, :, NOPE:NOPE + ROPE]).then_inc(mixw_full, 16)
                    for k in range(KVR // P):
                        sp.dma_start(wk_n[:, k * 256:(k + 1) * 256].rearrange("p (h c) -> p h c", h=HEADS),
                                     ukv[:, k, :, 0:NOPE]).then_inc(mixw_full, 16)
                        sp.dma_start(wk_v[:, k * 256:(k + 1) * 256].rearrange("p (h c) -> p h c", h=HEADS),
                                     ukv[:, k, :, NOPE:NOPE + MV]).then_inc(mixw_full, 16)
                    sp.dma_start(cos_m[:, :], t["k_cos_m"]).then_inc(mixw_full, 16)
                    sp.dma_start(sin_m[:, :], t["k_sin_m"]).then_inc(mixw_full, 16)
                    sp.dma_start(pool_inv[:, :], t["k_pool_inv"]).then_inc(counts_full, 16)
                    sp.wait_ge(poolw_zero, L + 1)
                    for g in range(len(WINDOWS)):
                        e = 64 * (g % 2)
                        sp.dma_start(pool_w[e:e + 64, (g // 2) * P + e:(g // 2) * P + e + 64],
                                     t["pool_w"][L][g]).then_inc(poolw_full, 16)
            for a in range(SEQ // P):
                sp.wait_ge(fin_out, a + 1)
                sp.dma_start(out[0][a * P:(a + 1) * P, :], x_tok[:, a * D:(a + 1) * D]).then_inc(stored, 16)
            sp.wait_ge(stored, 16 * (SEQ // P))

        @block.tensor
        def _(pe):
            pe.wait_ge(c_full, 16 * 3)
            pe.transpose(pair[2][:, 0:2 * KD], c_rows[0:2 * KD, :], ident[0:2 * KD, 0:2 * KD]).then_inc(c_done, 1)
            for k in range(KD):
                if k == 0:
                    pe.wait_ge(x_full, 16 * (TOK // P))
                if k >= 2:
                    pe.wait_ge(xt_out[k % 2], k // 2)
                for a in range(TOK // P):
                    mm = pe.transpose(pair[k % 2][:, a * P:(a + 1) * P], x_tok[:, a * D + k * P:a * D + (k + 1) * P],
                                      ident[:, :])
                mm.then_inc(xt_done, 1)
            pe.wait_ge(small_full, 16 * N_SMALL)
            pe.wait_ge(ones_ready, 1)
            for L in range(DEPTH):
                pe.transpose(pair[3][:, L * P:L * P + UNITS_MOD], rows[0:UNITS_MOD, L * P:(L + 1) * P],
                             ident[0:UNITS_MOD, 0:UNITS_MOD])
            pe.transpose(pair[3][:, 2 * P:2 * P + G_ROWS], rows[0:G_ROWS, 2 * P:3 * P], ident[0:G_ROWS, 0:G_ROWS])
            pe.matmul(pair[3][:, 512:1024], ones[0:1, :], lam_row[0:1, :], start=True, stop=True).then_inc(cols_done, 1)

            def first_mod():
                pe.wait_ge(silu_ready, 2)
                for m, src in enumerate((pro_w1, pro_w2)):
                    pe.wait_ge(pro_full[m], 16)
                    for a in range(0, D, 512):
                        for k in range(KD):
                            mm = pe.matmul(pair[m][0:2, a:a + 512], silu_c[:, 2 * k:2 * k + 2],
                                           src[:, k * D + a:k * D + a + 512], start=(k == 0), stop=(k == KD - 1))
                    mm.then_inc(mrow_done, 1)
                for m in range(2):
                    pe.wait_ge(mrow_out[m], 1)
                    for u in range(m * KD, (m + 1) * KD):
                        mm = pe.transpose(pair[2][:, 2 * u:2 * u + 2], mod_rows[0:2, u * P:(u + 1) * P], ident[0:2, 0:2])
                mm.then_inc(mod_done, 1)

            cnt = dict(sq=0, std=0, batch=1, n=0, h=0, s=[0, 0], step=0, oact=0, mix=0)

            def sum_squares(n_tiles, w_cols, dst):
                if cnt["std"]:
                    pe.wait_ge(std_ready, cnt["std"])
                for k in range(n_tiles):
                    pe.wait_ge(sq_ready, cnt["sq"] + 1)
                    for a, m in halves(w_cols):
                        mm = pe.matmul(dst[:, a:a + m], ones[:, :], sq_src(cnt["sq"])[:, a:a + m],
                                       start=(k == 0), stop=(k == n_tiles - 1))
                    mm.then_inc(sq_used, 1)
                    cnt["sq"] += 1
                cnt["std"] += 1

            def sq_src(n):
                return sq[n % 2]

            def unit(w, i, s, first):
                hi, lo = hi_w[s], lo_w[s]
                src_hi, src_lo = (h_hi, h_lo) if w["what"].endswith("_down") else (n_hi, n_lo)
                pe.wait_ge(lo_ready[s], w["base"] + i + 1)
                if not (first and w["base"] == 0):
                    pe.wait_ge(pair_free[s], w["base"] + i)
                for k in range(w["kt"]):
                    if w["what"].endswith("_down"):
                        pe.wait_ge(h_ready, cnt["h"] + k + 1)
                    elif w["what"] == "out":
                        pe.wait_ge(mix_ready, cnt["mix"])
                    else:
                        pe.wait_ge(n_ready, cnt["n"] + k + 1)
                    for wt, src in ((hi, src_hi), (hi, src_lo), (lo, src_hi)):
                        for a, m in halves(width(w, s)):
                            mm = pe.matmul(pair[s][:, a:a + m], wt[:, k * P:(k + 1) * P], tile(src, k, m, a),
                                           start=(k == 0 and wt is hi and src is src_hi),
                                           stop=(k == w["kt"] - 1 and wt is lo))
                mm.then_inc(unit_done[s], 1)

            def mod_tiles(w, i):
                b = cnt["batch"] + i
                pe.wait_ge(mod_sum, 2 * KD * b)
                pe.wait_ge(mod_out, b)
                for m in range(MOD_T):
                    for e in range(2):
                        mm = pe.matmul(pair[2][:, (2 * m + e) * P:(2 * m + e + 1) * P],
                                       mod_acc[:, e * MOD_W + m * P:e * MOD_W + (m + 1) * P], ones[:, :],
                                       start=True, stop=True)
                mm.then_inc(mod_done, 1)

            def sweep(w):
                per = mod_tile(w) is not None
                unit(w, 0, 0, True)
                unit(w, 0, 1, True)
                if per:
                    mod_tiles(w, 0)
                if w["n"] > 1:
                    with pe.Fori(1, w["n"]) as i:
                        unit(w, i, 0, False)
                        unit(w, i, 1, False)
                        if per:
                            mod_tiles(w, i)
                if per:
                    cnt["batch"] += w["n"]

            def mixer(L):
                w_last = [w for w in SWEEPS if w["layer"] == L and w["what"] == "in"][-1]
                more = L < DEPTH - 1
                nq_all = TOK if more else SEQ
                for s in range(2):
                    pe.wait_ge(pair_free[s], w_last["base"] + w_last["n"])
                pe.wait_ge(mod_out, cnt["batch"])

                def task_start(a):
                    if a >= 3:
                        who = TASKS[a - 3][2]
                        freed, each = (out_act, N_ACT) if who == "a" else (out_dve, N_DVE)
                        pe.wait_ge(freed, L * each + read_out(who, a - 2))
                    return pair[a % 3]

                sum_squares(2, TOK, pair[3])
                for a, (what, arg, _) in enumerate(TASKS):
                    if a == 3:
                        sum_squares(3, nq_all, pair[3])
                    if what == "vm" and arg == 0:
                        pe.wait_ge(mixw_full, 16 * 12 * (L + 1))
                        pe.wait_ge(applied, 2 * L + 1)
                    if what == "uq" and arg == 0:
                        pe.wait_ge(applied, 2 * L + 2)
                    if what == "rope" and arg == T_DQ:
                        pe.wait_ge(tables_full, 16 * 4)
                    if what == "rope" and arg == T_Q + 2:
                        pe.wait_ge(out_act, L * N_ACT + read_out("a", a))
                    dst = task_start(a)
                    if what == "v":
                        for j in range(HEADS):
                            mm = pe.transpose(dst[:, j * P:(j + 1) * P], tile(proj, T_DV + j, P, arg * P), ident[:, :])
                    elif what == "rope":
                        perm = perm_d if T_DQ <= arg < T_DV else perm_m
                        mm = pe.matmul(dst[:, 0:SEQ], perm[:, :], tile(proj, arg, SEQ), start=True, stop=True)
                    elif what == "vm":
                        for e in range(2):
                            for k in range(2):
                                mm = pe.matmul(dst[:, e * 512:e * 512 + 256], tile(proj, T_KV + k, P, (2 * arg + e) * P),
                                               wk_v[:, k * 256:(k + 1) * 256], start=(k == 0), stop=(k == 1))
                    elif what == "kn":
                        for b, m in halves(TOK):
                            for k in range(2):
                                mm = pe.matmul(dst[:, b:b + m], wk_n[:, k * 256 + arg * P:k * 256 + (arg + 1) * P],
                                               tile(proj, T_KV + k, m, b), start=(k == 0), stop=(k == 1))
                    else:
                        for b, m in halves(nq_all):
                            for k in range(3):
                                lhs = (wq_n[:, k * 256 + arg * P:k * 256 + (arg + 1) * P] if arg < 2
                                       else wq_r[:, k * P:(k + 1) * P])
                                mm = pe.matmul(dst[:, b:b + m], lhs, tile(proj, T_Q + k, m, b),
                                               start=(k == 0), stop=(k == 2))
                    mm.then_inc(task_done, 1)
                pe.wait_ge(out_act, (L + 1) * N_ACT)
                pe.wait_ge(out_dve, (L + 1) * N_DVE)
                pe.wait_ge(std_ready, cnt["std"])

                steps = steps_of(L)

                def scores(n, kind, h, q0, k0, nk, s):
                    if cnt["s"][s]:
                        pe.wait_ge(exp_done[s], cnt["s"][s])
                    for a, m in halves(nk):
                        if kind == "diff":
                            e = 64 * s
                            mm = pe.matmul(pair[s][:, a:a + m], tile(proj, T_DQ + h, P, q0)[e:e + 64, :],
                                           tile(proj, T_DK + h, m, k0 + a)[e:e + 64, :], start=True, stop=True)
                        else:
                            e, r = 64 * (h % 2), 32 * h
                            pe.matmul(pair[s][:, a:a + m], tile(proj, T_Q + h // 2, P, q0)[e:e + 64, :],
                                      tile(proj, T_KV + h // 2, m, k0 + a)[e:e + 64, :], start=True, stop=False)
                            mm = pe.matmul(pair[s][:, a:a + m], tile(proj, T_Q + 2, P, q0)[r:r + 32, :],
                                           tile(proj, T_KR, m, k0 + a)[r:r + 32, :], start=False, stop=True,
                                           tile_position=(r, 0))
                    mm.then_inc(s_ready[s], 1)
                    cnt["s"][s] += 1

                st0 = cnt["step"]
                for n in range(len(steps) + 1):
                    if n < len(steps):
                        (kind, h, q0, nq, k0, nk), gi, b = steps[n]
                        if kind == "diff":
                            for s in range(2):
                                scores(n, kind, h, q0 + b * P, k0, nk, s)
                        else:
                            scores(n, kind, h, q0 + b * P, k0, nk, n % 2)
                    if n == 0:
                        continue
                    (kind, h, q0, nq, k0, nk), gi, b = steps[n - 1]
                    src = buf[step_buf(L, n - 1)]
                    pe.wait_ge(p_ready, st0 + n)
                    if st0 + n - 1:
                        pe.wait_ge(pt_ready, st0 + n - 1)
                    for a in range(nk // P):
                        mm = pe.transpose(pair[2][:, a * P:(a + 1) * P], src[:, a * P:(a + 1) * P], ident[:, :])
                    mm.then_inc(t_done, 1)
                    if b < nq // P - 1:
                        continue
                    pe.wait_ge(pt_ready, st0 + n)
                    if kind == "diff":
                        if cnt["oact"]:
                            pe.wait_ge(o_act, cnt["oact"])
                        cnt["oact"] += 1
                    else:
                        m = gi - N_DIFF[L]
                        if m == 0:
                            pe.wait_ge(o_act, cnt["oact"])
                        elif m % 2 == 0:
                            pe.wait_ge(mix_ready, sum(MIX_OF[:L]) + m - 1 + m // 2)
                    for a in range(nk // P):
                        kt = k0 // P + a
                        if kind == "diff":
                            mm = pe.matmul(pair[3][:, 0:nq], v_tok[:, kt * 512 + h * P:kt * 512 + (h + 1) * P],
                                           p_t[:, a * 512:a * 512 + nq], start=(a == 0), stop=(a == nk // P - 1))
                        else:
                            e = 64 * (h % 2)
                            mm = pe.matmul(pair[3][e:e + 64, 0:nq], v_mla[:, kt * 256 + h * MV:kt * 256 + (h + 1) * MV],
                                           p_t[:, a * 512:a * 512 + nq], start=(a == 0), stop=(a == nk // P - 1))
                    mm.then_inc(pv_done, 1)
                    if kind == "mla":
                        dg = GROUPS_OF[L][gi - N_DIFF[L]]
                        pe.wait_ge(std_ready, cnt["std"])
                        pe.wait_ge(sq_ready, cnt["sq"] + 1)
                        pe.matmul(pair[3][:, 512:512 + dg[3]], ones[:, :], tile(proj, T_DK, dg[3]),
                                  start=True, stop=True).then_inc(sq_used, 1)
                        cnt["sq"] += 1
                        cnt["std"] += 1
                cnt["step"] += len(steps)
                pe.wait_ge(pool_ready, 2 * (L + 1))
                pe.wait_ge(poolw_full, 16 * len(WINDOWS) * (L + 1))
                for a in range(2):
                    pe.wait_ge(exp_done[a], cnt["s"][a])
                    for b, m in halves(nq_all):
                        mm = pe.matmul(pair[a][:, b:b + m], pool_w[:, a * P:(a + 1) * P], tile(proj, T_POOL + a, m, b),
                                       start=True, stop=True)
                    mm.then_inc(poolmm_done, 1)
                cnt["mix"] = sum(MIX_OF[:L + 1])

            for q, w in enumerate(SWEEPS):
                if w["arg"] == 0 and w["what"] in ("ffn1_up", "ffn2_up", "in"):
                    if q == 0:
                        for e in range(2):
                            pe.wait_ge(xt_out[e], KD // 2)
                        pe.wait_ge(cols_out, 1)
                    sum_squares(KD, norm_width(w), pair[3])
                    if q == 0:
                        first_mod()
                if w["what"] == "out":
                    mixer(w["layer"])
                sweep(w)
                if w["what"] == "in" and w["arg"] == 12 or w["what"].endswith("_up") and w["arg"] == 1:
                    cnt["n"] += KD
                if w["what"].endswith("_down"):
                    cnt["h"] += FG
            sum_squares(KD, SEQ, pair[3])
            pe.wait_ge(n_ready, cnt["n"] + KD)
            for a in range(SEQ // P):
                if a < 2:
                    pe.wait_ge(pair_free[a], SWEEPS[-1]["base"] + SWEEPS[-1]["n"])
                else:
                    pe.wait_ge(fin_out, a - 1)
                for k in range(KD):
                    mm = pe.transpose(pair[a % 2][:, k * P:(k + 1) * P], tile(x, k, P, a * P), ident[:, :])
                mm.then_inc(fin_done, 1)

        @block.scalar
        def _(act):
            act.wait_ge(c_done, 1)
            for e in range(2):
                act.activation(silu_c[:, e:2 * KD:2], pair[2][:, e * KD:(e + 1) * KD], ACT.Silu).then_inc(silu_ready, 1)
            for k in range(0, KD, 2):
                act.wait_ge(xt_done, k + 1)
                act.copy(tile(x, k), pair[0][:, 0:TOK]).then_inc(xt_out[0], 1)
            act.wait_ge(lam_ready, 1)
            act.activation(lam_exp[:, :], lam_sum[:, :], ACT.Exp).then_inc(lam_ready, 1)

            cnt = dict(sq=0, std=0, used=None, n=0, step=0, s=0, group=0, otmp=0)

            def split_hi(w, i, s, first):
                act.wait_ge(raw_full[s], (w["base"] + i + 1) * 16)
                if is_krope(w, s):
                    act.wait_ge(krope_full, 16 * (HEADS - 1) * (w["layer"] + 1))
                if not (first and w["base"] == 0):
                    act.wait_ge(unit_done[s], w["base"] + i)
                act.copy(hi_w[s][:, 0:w["kt"] * P], raw_w[s][:, 0:w["kt"] * P]).then_inc(hi_ready[s], 1)

            def square(src, w_cols, dst=None):
                if cnt["sq"] >= 2:
                    act.wait_ge(sq_used, cnt["sq"] - 1)
                act.activation((sq[cnt["sq"] % 2] if dst is None else dst)[:, 0:w_cols], src, ACT.Square)\
                   .then_inc(sq_ready, 1)
                cnt["sq"] += 1

            def std(src, w_cols, n):
                act.wait_ge(sq_used, cnt["sq"])
                if cnt["used"]:
                    act.wait_ge(*cnt["used"])
                cnt["std"] += 1
                act.activation(rstd[:, 0:w_cols], src[:, 0:w_cols], ACT.Ln, bias=eps_col[:, 0:1], scale=1.0 / n)\
                   .then_inc(log_ready, 1)
                act.wait_ge(log_ready, cnt["std"])
                act.activation(rstd[:, 0:w_cols], rstd[:, 0:w_cols], ACT.Exp, scale=-0.5).then_inc(std_ready, 1)

            def norm_x(w_cols, wait_tile, shift):
                for k in range(KD):
                    wait_tile(k)
                    square(tile(x, k, w_cols), w_cols)
                std(pair[3], w_cols, D)
                if shift is None:
                    return
                if cnt["n"] == 0:
                    act.wait_ge(mrow_done, 1)
                    act.copy(mod_rows[0:2, 0:D], pair[0][0:2, :]).then_inc(mrow_out[0], 1)
                for k in range(KD):
                    act.wait_ge(t_ready, cnt["n"] + k + 1)
                    for e, (a, m) in enumerate(halves(w_cols)):
                        ins = act.activation(tile(n_hi, k, m, a), buf[k % 2][:, a:a + m], ACT.Identity,
                                             bias=mod[:, shift + 2 * k + e:shift + 2 * k + e + 1])
                    ins.then_inc(nhi_ready, 1)
                cnt["n"] += KD
                cnt["used"] = (t_ready, cnt["n"])

            def finish(w, i, s):
                n, what = w["base"] + i + 1, w["what"]
                if what.endswith("_up"):
                    if s == 0:
                        act.wait_ge(unit_done[0], n)
                        if not (isinstance(n, int) and n == 1):
                            act.wait_ge(pair_free[1], n - 1)
                        act.activation(act_buf[:, 0:width(w, 0)], pair[0][:, 0:width(w, 0)], ACT.Silu)\
                           .then_inc(pair_free[0], 1)
                    else:
                        act.wait_ge(pair_free[1], n)
                        act.copy(tile(h_hi, i, width(w, 1)), hid_buf[:, 0:width(w, 1)]).then_inc(hhi_ready, 1)
                elif what == "in" and s == 0:
                    act.wait_ge(unit_done[0], n)
                    act.copy(tile(proj, w["arg"] + 2 * i, width(w, 0)), pair[0][:, 0:width(w, 0)])\
                       .then_inc(pair_free[0], 1)

            def sweep(q):
                w = SWEEPS[q]
                if q == 0:
                    split_hi(w, 0, 0, True)
                split_hi(w, 0, 1, True)
                finish(w, 0, 0)
                if w["n"] > 1:
                    with act.Fori(1, w["n"]) as i:
                        split_hi(w, i, 0, False)
                        finish(w, i - 1, 1)
                        split_hi(w, i, 1, False)
                        finish(w, i, 0)
                if q + 1 < len(SWEEPS):
                    split_hi(SWEEPS[q + 1], 0, 0, True)
                finish(w, w["n"] - 1, 1)

            def mixer(L):
                w_last = [w for w in SWEEPS if w["layer"] == L and w["what"] == "in"][-1]
                more = L < DEPTH - 1
                nq_all = TOK if more else SEQ
                act.wait_ge(pair_free[1], w_last["base"] + w_last["n"])
                act.wait_ge(pair_free[0], w_last["base"] + w_last["n"])
                for k in range(2):
                    square(tile(proj, T_KV + k), TOK)
                std(pair[3], TOK, KVR)
                cnt["used"] = (applied, 2 * L + 1)
                for a, (what, arg, who) in enumerate(TASKS):
                    if a == 3:
                        for k in range(3):
                            square(tile(proj, T_Q + k, nq_all), nq_all)
                        std(pair[3], nq_all, QR)
                        cnt["used"] = (applied, 2 * L + 2)
                    if who != "a":
                        continue
                    last = {"kn": 1, "uq": 2}.get(what, arg)
                    act.wait_ge(task_done, L * len(TASKS) + a + 1 + last - arg)
                    src = pair[a % 3]
                    if what == "v":
                        ins = act.copy(v_tok[:, arg * 512:(arg + 1) * 512], src[:, 0:512])
                    elif what == "vm":
                        ins = act.copy(v_mla[:, arg * 512:(arg + 1) * 512].rearrange("p (e c) -> p e c", e=2),
                                       src[:, :].rearrange("p (e c) -> p e c", e=2)[:, :, 0:256])
                    elif what == "kn":
                        ins = act.copy(tile(proj, T_KV + arg), src[:, 0:TOK])
                    else:
                        ins = act.copy(tile(proj, T_Q + arg, nq_all), src[:, 0:nq_all])
                    ins.then_inc(out_act, 1)

                steps = steps_of(L)
                st0 = cnt["step"]
                for n in range(len(steps) + 1):
                    if n < len(steps):
                        (kind, h, q0, nq, k0, nk), gi, b = steps[n]
                        if n >= 2:
                            act.wait_ge(t_done, st0 + n - 1)
                        else:
                            act.wait_ge(out_dve, (L + 1) * N_DVE)
                        for s in ((0, 1) if kind == "diff" else (n % 2,)):
                            c = cnt["s"]
                            act.wait_ge(max_ready, c + 1)
                            act.activation(buf[step_buf(L, n) + (s if kind == "diff" else 0)][:, 0:nk], pair[s][:, 0:nk],
                                           ACT.Exp, bias=max_bias[:, c % 8:c % 8 + 1],
                                           scale=SC_DIFF if kind == "diff" else SC_MLA,
                                           accum_out=exp_sum[:, c % 8:c % 8 + 1]).then_inc(exp_done[s], 1)
                            cnt["s"] += 1
                    if n == 0:
                        continue
                    (kind, h, q0, nq, k0, nk), gi, b = steps[n - 1]
                    act.wait_ge(t_done, st0 + n)
                    if b == 0 and cnt["group"]:
                        act.wait_ge(pv_done, cnt["group"])
                    act.copy(p_t[:, 0:(nk // P) * 512].rearrange("p (a c) -> p a c", c=512)[:, :, b * P:(b + 1) * P],
                             pair[2][:, 0:nk].rearrange("p (a c) -> p a c", c=P)).then_inc(pt_ready, 1)
                    if b < nq // P - 1:
                        continue
                    cnt["group"] += 1
                    act.wait_ge(pv_done, cnt["group"])
                    if kind == "diff":
                        act.copy(tile(proj, T_DQ + h, nq, q0), pair[3][:, 0:nq]).then_inc(o_act, 1)
                        continue
                    if gi == N_DIFF[L]:
                        act.wait_ge(pool_ready, 2 * (L + 1))
                    if h % 2:
                        act.copy(tile(n_hi, M_MLA + h // 2, nq, q0), pair[3][:, 0:nq]).then_inc(mhi_ready, 1)
                    _, dh, dq, dn, _, _ = GROUPS_OF[L][gi - N_DIFF[L]]
                    if gi == N_DIFF[L]:
                        act.wait_ge(o_act, sum(N_DIFF[:L + 1]))
                    square(tile(proj, T_DQ + dh, dn, dq), dn, tile(proj, T_DK, dn))
                    std(pair[3][:, 512:1024], dn, 2 * DDIM)
                    cnt["otmp"] += 1
                    cnt["used"] = (otmp_ready, cnt["otmp"])
                    act.wait_ge(otmp_ready, cnt["otmp"])
                    act.copy(tile(n_hi, M_DIFF + dh, dn, dq), tile(proj, T_DK + 1, dn)).then_inc(mhi_ready, 1)
                cnt["step"] += len(steps)
                for a in range(2):
                    act.wait_ge(poolmm_done, 2 * L + a + 1)
                    g = L * G_LAYER + G_POOL + a
                    act.activation(tile(n_hi, M_POOL + a, nq_all), pair[a][:, 0:nq_all], ACT.Identity,
                                   scale=gains[:, g:g + 1]).then_inc(mhi_ready, 1)

            act.wait_ge(cols_out, 1)
            for q, w in enumerate(SWEEPS):
                if w["arg"] == 0 and w["what"] in ("ffn1_up", "ffn2_up", "in"):
                    chunk = {"ffn1_up": 0, "in": 3, "ffn2_up": 6}[w["what"]]

                    def wait_tile(k):
                        if q == 0:
                            act.wait_ge(xt_out[k % 2], k // 2 + 1)
                        else:
                            act.wait_ge(pair_free[k % 2], SWEEPS[q - 1]["base"] + k // 2 + 1)
                    norm_x(norm_width(w), wait_tile, mod_col(w["layer"], chunk))
                if w["what"] == "out":
                    mixer(w["layer"])
                sweep(q)
            last = SWEEPS[-1]
            norm_x(SEQ, lambda k: act.wait_ge(pair_free[k % 2], last["base"] + k // 2 + 1), None)
            for a in range(0, SEQ // P):
                act.wait_ge(fin_done, a + 1)
                act.copy(x_tok[:, a * D:(a + 1) * D], pair[a % 2][:, :]).then_inc(fin_out, 1)

        @block.vector
        def _(dve):
            links = 0

            def link(ins):
                nonlocal links
                links += 1
                ins.then_inc(dve_chain, 1)
                dve.wait_ge(dve_chain, links)

            dve.memset(eps_col[:, :], EPS)
            dve.memset(ones[:, :], 1.0).then_inc(ones_ready, 1)
            for k in range(1, KD, 2):
                dve.wait_ge(xt_done, k + 1)
                dve.tensor_copy(tile(x, k), pair[1][:, 0:TOK]).then_inc(xt_out[1], 1)
            dve.wait_ge(cols_done, 1)
            dve.tensor_copy(b_mod[:, 0:UNITS_MOD], pair[3][:, 0:UNITS_MOD])
            dve.tensor_copy(b_mod[:, UNITS_MOD:], pair[3][:, P:P + UNITS_MOD])
            dve.tensor_copy(gains[:, :], pair[3][:, 2 * P:2 * P + G_ROWS])
            link(dve.tensor_copy(lam_prod[:, 0:512], pair[3][:, 512:1024]))
            lv = lam_prod[:, 0:512].rearrange("p (l two d) -> p l two d", two=2, d=DDIM)
            products = lam_prod[:, 512:768].rearrange("p (l d) -> p l d", d=DDIM)
            dve.tensor_tensor(products, lv[:, :, 0, :], lv[:, :, 1, :], ALU.mult).then_inc(cols_out, 1)
            dve.wait_ge(cols_out, 1)
            dve.tensor_reduce(lam_sum[:, :], products, AX.X, ALU.add).then_inc(lam_ready, 1)
            dve.wait_ge(lam_ready, 2)
            for L in range(DEPTH):
                link(dve.tensor_tensor(neg_lam[:, L:L + 1], lam_exp[:, 2 * L + 1:2 * L + 2], lam_exp[:, 2 * L:2 * L + 1],
                                       ALU.subtract))
                link(dve.tensor_scalar(neg_lam[:, L:L + 1], neg_lam[:, L:L + 1], -LAM_INIT[L], None, ALU.add))
                g = L * G_LAYER + G_SUB
                link(dve.tensor_scalar(sub_gain[:, L:L + 1], gains[:, g:g + 1], 1.0 - LAM_INIT[L], None, ALU.mult))
            cnt = dict(std=0, n=0, h=0, batch=1, s=0, sp=[0, 0], mhi=0, mix=0)

            def split_lo(w, i, s):
                dve.wait_ge(hi_ready[s], w["base"] + i + 1)
                m = w["kt"] * P
                dve.tensor_tensor(lo_w[s][:, 0:m], raw_w[s][:, 0:m], hi_w[s][:, 0:m].bitcast(F32), ALU.subtract)\
                   .then_inc(lo_ready[s], 1)

            def wait_rstd():
                dve.wait_ge(std_ready, cnt["std"] + 1)
                cnt["std"] += 1

            def norm_x(w_cols, L, gain, shift):
                parts = list(enumerate(halves(w_cols)))
                if cnt["n"] == 0:
                    dve.wait_ge(mrow_done, 2)
                    dve.tensor_copy(mod_rows[0:2, D:2 * D], pair[1][0:2, :]).then_inc(mrow_out[1], 1)
                    dve.wait_ge(mod_done, 1)
                    for e in range(2):
                        ins = dve.tensor_tensor(mod[:, e:2 * PRO_UNITS:2], pair[2][:, e:2 * PRO_UNITS:2],
                                                b_mod[:, 0:PRO_UNITS], ALU.add)
                    ins.then_inc(mod_out, 1)
                dve.wait_ge(mod_out, cnt["batch"])
                for e in range(2):
                    ins = dve.scalar_tensor_tensor(out=scale_a[:, e:16:2], in0=mod[:, shift + 16 + e:shift + 32:2], scalar=1.0,
                                                   in1=gains[:, gain:gain + KD], op0=ALU.add, op1=ALU.mult)
                link(ins)
                wait_rstd()

                def low(k):
                    dve.wait_ge(nhi_ready, cnt["n"] + k + 1)
                    for e, (a, m) in parts:
                        ins = dve.scalar_tensor_tensor(out=tile(n_lo, k, m, a), in0=buf[k % 2][:, a:a + m],
                                                       scalar=mod[:, shift + 2 * k + e:shift + 2 * k + e + 1],
                                                       in1=tile(n_hi, k, m, a).bitcast(F32), op0=ALU.add, op1=ALU.subtract)
                    ins.then_inc(n_ready, 1)

                for k in range(KD):
                    if k >= 2:
                        dve.wait_ge(n_ready, cnt["n"] + k - 1)
                    for e, (a, m) in parts:
                        ins = dve.scalar_tensor_tensor(out=buf[k % 2][:, a:a + m], in0=tile(x, k, m, a),
                                                       scalar=scale_a[:, 2 * k + e:2 * k + e + 1],
                                                       in1=rstd[:, a:a + m], op0=ALU.mult, op1=ALU.mult)
                    ins.then_inc(t_ready, 1)
                    if k:
                        low(k - 1)
                low(KD - 1)
                cnt["n"] += KD

            def finish(w, i, s):
                n, what = w["base"] + i + 1, w["what"]
                if what.endswith("_up"):
                    if s == 1:
                        m = width(w, 1)
                        dve.wait_ge(unit_done[1], n)
                        dve.wait_ge(pair_free[0], n)
                        if not (isinstance(i, int) and cnt["h"] + i == 0):
                            dve.wait_ge(h_ready, cnt["h"] + i)
                        dve.tensor_tensor(hid_buf[:, 0:m], pair[1][:, 0:m], act_buf[:, 0:m], ALU.mult)\
                           .then_inc(pair_free[1], 1)
                        dve.wait_ge(hhi_ready, cnt["h"] + i + 1)
                        dve.tensor_tensor(tile(h_lo, i, m), hid_buf[:, 0:m], tile(h_hi, i, m).bitcast(F32), ALU.subtract)\
                           .then_inc(h_ready, 1)
                elif what == "in":
                    if s == 1:
                        dve.wait_ge(unit_done[1], n)
                        dve.tensor_copy(tile(proj, w["arg"] + 2 * i + 1, width(w, 1)), pair[1][:, 0:width(w, 1)])\
                           .then_inc(pair_free[1], 1)
                else:
                    dve.wait_ge(unit_done[s], n)
                    for e, (a, m) in enumerate(halves(width(w, s))):
                        xs = tile(x, 2 * i + s, m, a)
                        ins = dve.scalar_tensor_tensor(out=xs, in0=pair[s][:, a:a + m],
                                                       scalar=gate[:, bass.ds((2 * i + s) * 2 + e, 1)], in1=xs,
                                                       op0=ALU.mult, op1=ALU.add)
                    ins.then_inc(pair_free[s], 1)

            def mod_add(w, i):
                b = cnt["batch"] + i
                dve.wait_ge(mod_full, b * 16)
                dve.wait_ge(mod_done, b)
                for k in range(KD):
                    for e in range(2):
                        acc, part = mod_acc[:, e * MOD_W:(e + 1) * MOD_W], mod_w[:, k * MOD_W:(k + 1) * MOD_W]
                        gain = silu_c[:, 2 * k + e:2 * k + e + 1]
                        if k == 0:
                            ins = dve.tensor_scalar(acc, part, gain, None, ALU.mult)
                        else:
                            dve.wait_ge(mod_sum, 2 * KD * (b - 1) + 2 * k + e - 1)
                            ins = dve.scalar_tensor_tensor(out=acc, in0=part, scalar=gain, in1=acc,
                                                           op0=ALU.mult, op1=ALU.add)
                        ins.then_inc(mod_sum, 1)

            def mod_evict(w, i):
                b = cnt["batch"] + i
                dve.wait_ge(mod_done, b + 1)
                for m in range(MOD_T):
                    u = mod_tile(w) + MOD_T * i + m
                    ins = dve.tensor_scalar(mod[:, bass.ds(u * 2, 2)], pair[2][:, 2 * m * P:2 * (m + 1) * P:P],
                                            b_mod[:, bass.ds(u, 1)], None, ALU.add)
                ins.then_inc(mod_out, 1)

            def sweep(q):
                w = SWEEPS[q]
                per = mod_tile(w) is not None
                if q == 0:
                    split_lo(w, 0, 0)
                split_lo(w, 0, 1)
                if per:
                    mod_add(w, 0)
                finish(w, 0, 0)
                if w["n"] > 1:
                    with dve.Fori(1, w["n"]) as i:
                        split_lo(w, i, 0)
                        finish(w, i - 1, 1)
                        split_lo(w, i, 1)
                        if per:
                            mod_evict(w, i - 1)
                            mod_add(w, i)
                        finish(w, i, 0)
                if q + 1 < len(SWEEPS):
                    split_lo(SWEEPS[q + 1], 0, 0)
                finish(w, w["n"] - 1, 1)
                if per:
                    mod_evict(w, w["n"] - 1)
                    cnt["batch"] += w["n"]
                if w["what"].endswith("_up"):
                    cnt["h"] += FG

            def rotate(L, a, arg):
                c, s = (cos_d, sin_d) if T_DQ <= arg < T_DV else (cos_m, sin_m)
                dve.wait_ge(task_done, L * len(TASKS) + a + 1)
                dve.wait_ge(out_dve, L * N_DVE + read_out("d", a))
                dve.tensor_tensor(buf[0][:, 0:SEQ], pair[a % 3][:, 0:SEQ], s[:, :], ALU.mult)
                link(dve.tensor_tensor(buf[1][:, 0:SEQ], tile(proj, arg, SEQ), c[:, :], ALU.mult))
                dve.tensor_tensor(tile(proj, arg, SEQ), buf[0][:, 0:SEQ], buf[1][:, 0:SEQ], ALU.add).then_inc(out_dve, 1)

            def mixer(L):
                w_last = [w for w in SWEEPS if w["layer"] == L and w["what"] == "in"][-1]
                more = L < DEPTH - 1
                nq_all = TOK if more else SEQ

                def apply(t0, nt, gain, m):
                    wait_rstd()
                    for k in range(nt):
                        ins = dve.scalar_tensor_tensor(out=tile(proj, t0 + k, m), in0=tile(proj, t0 + k, m),
                                                       scalar=gains[:, L * G_LAYER + gain + k:L * G_LAYER + gain + k + 1],
                                                       in1=rstd[:, 0:m], op0=ALU.mult, op1=ALU.mult)
                    ins.then_inc(applied, 1)

                apply(T_KV, 2, G_KVN, TOK)
                for a, (what, arg, who) in enumerate(TASKS):
                    if a == 5:
                        apply(T_Q, 3, G_QN, nq_all)
                    if who != "d":
                        continue
                    if what == "v":
                        dve.wait_ge(task_done, L * len(TASKS) + a + 1)
                        dve.tensor_copy(v_tok[:, arg * 512:(arg + 1) * 512], pair[a % 3][:, 0:512]).then_inc(out_dve, 1)
                    else:
                        if arg == T_DQ:
                            dve.wait_ge(tables_full, 16 * 4)
                        if arg == T_KR:
                            dve.wait_ge(mixw_full, 16 * 12 * (L + 1))
                        rotate(L, a, arg)

                steps = steps_of(L)
                for n, ((kind, h, q0, nq, k0, nk), gi, b) in enumerate(steps):
                    pairs = (0, 1) if kind == "diff" else (n % 2,)
                    scale = SC_DIFF if kind == "diff" else SC_MLA
                    c0 = cnt["s"]
                    for s in pairs:
                        c = cnt["s"] % 8
                        dve.wait_ge(s_ready[s], cnt["sp"][s] + 1)
                        link(dve.tensor_reduce(neg_max[:, c:c + 1], pair[s][:, 0:nk], AX.X, ALU.max, negate=True))
                        dve.tensor_scalar(max_bias[:, c:c + 1], neg_max[:, c:c + 1], scale, None, ALU.mult)\
                           .then_inc(max_ready, 1)
                        cnt["s"] += 1
                        cnt["sp"][s] += 1
                    e0 = step_buf(L, n)
                    for s in pairs:
                        dve.wait_ge(exp_done[s], cnt["sp"][s])
                    c = c0 % 8
                    m = len(pairs)
                    link(dve.reciprocal(inv_sum[:, c:c + m], exp_sum[:, c:c + m]))
                    if kind == "diff":
                        dve.tensor_scalar(inv_sum[:, c + 1:c + 2], inv_sum[:, c + 1:c + 2], neg_lam[:, L:L + 1], None,
                                          ALU.mult)
                        link(dve.tensor_scalar(buf[e0][:, 0:nk], buf[e0][:, 0:nk], inv_sum[:, c:c + 1], None, ALU.mult))
                        dve.scalar_tensor_tensor(out=buf[e0][:, 0:nk], in0=buf[e0 + 1][:, 0:nk],
                                                 scalar=inv_sum[:, c + 1:c + 2], in1=buf[e0][:, 0:nk],
                                                 op0=ALU.mult, op1=ALU.add).then_inc(p_ready, 1)
                    else:
                        dve.tensor_scalar(buf[e0][:, 0:nk], buf[e0][:, 0:nk], inv_sum[:, c:c + 1], None, ALU.mult)\
                           .then_inc(p_ready, 1)
                    if n:
                        group_end(L, steps[n - 1])
                group_end(L, steps[-1])
                for a in range(2):
                    cnt["mhi"] += 1
                    dve.wait_ge(mhi_ready, cnt["mhi"])
                    g = L * G_LAYER + G_POOL + a
                    dve.scalar_tensor_tensor(out=tile(n_lo, M_POOL + a, nq_all), in0=pair[a][:, 0:nq_all],
                                             scalar=gains[:, g:g + 1], in1=tile(n_hi, M_POOL + a, nq_all).bitcast(F32),
                                             op0=ALU.mult, op1=ALU.subtract).then_inc(mix_ready, 1)

            def group_end(L, step):
                (kind, h, q0, nq, k0, nk), gi, b = step
                if b < nq // P - 1 or kind == "diff":
                    return
                if h % 2:
                    cnt["mhi"] += 1
                    dve.wait_ge(mhi_ready, cnt["mhi"])
                    dve.tensor_tensor(tile(n_lo, M_MLA + h // 2, nq, q0), pair[3][:, 0:nq],
                                      tile(n_hi, M_MLA + h // 2, nq, q0).bitcast(F32), ALU.subtract).then_inc(mix_ready, 1)
                _, dh, dq, dn, _, _ = GROUPS_OF[L][gi - N_DIFF[L]]
                wait_rstd()
                tmp = tile(proj, T_DK + 1, dn)
                if gi > N_DIFF[L]:
                    dve.wait_ge(mix_ready, cnt["mix"])
                dve.scalar_tensor_tensor(out=tmp, in0=tile(proj, T_DQ + dh, dn, dq), scalar=sub_gain[:, L:L + 1],
                                         in1=rstd[:, 0:dn], op0=ALU.mult, op1=ALU.mult).then_inc(otmp_ready, 1)
                cnt["mhi"] += 1
                dve.wait_ge(mhi_ready, cnt["mhi"])
                dve.tensor_tensor(tile(n_lo, M_DIFF + dh, dn, dq), tmp, tile(n_hi, M_DIFF + dh, dn, dq).bitcast(F32),
                                  ALU.subtract).then_inc(mix_ready, 1)
                cnt["mix"] = sum(MIX_OF[:L]) + gi - N_DIFF[L] + 1 + (gi - N_DIFF[L] + 1) // 2

            for q, w in enumerate(SWEEPS):
                L = w["layer"]
                if w["arg"] == 0 and w["what"] in ("ffn1_up", "ffn2_up", "in"):
                    chunk, gain = {"ffn1_up": (0, G_FFN1), "in": (3, G_MIX), "ffn2_up": (6, G_FFN2)}[w["what"]]
                    norm_x(norm_width(w), L, L * G_LAYER + gain, mod_col(L, chunk))
                if w["what"] == "out":
                    mixer(L)
                if w["arg"] == 0 and w["what"] in ("ffn1_down", "ffn2_down", "out"):
                    c = mod_col(L, {"ffn1_down": 2, "out": 5, "ffn2_down": 8}[w["what"]])
                    dve.wait_ge(mod_out, cnt["batch"])
                    link(dve.tensor_scalar(gate[:, :], mod[:, c:c + 16], 1.0 if w["what"] == "out" else 0.5, None, ALU.mult))
                sweep(q)
            wait_rstd()
            for k in range(KD):
                dve.scalar_tensor_tensor(out=tile(x, k, SEQ), in0=tile(x, k, SEQ), scalar=gains[:, G_FINAL + k:G_FINAL + k + 1],
                                         in1=rstd[:, 0:SEQ], op0=ALU.mult, op1=ALU.mult).then_inc(n_ready, 1)

        @block.gpsimd
        def _(pool):
            links = 0

            def link(ins):
                nonlocal links
                links += 1
                ins.then_inc(pool_chain, 1)
                pool.wait_ge(pool_chain, links)

            def window_sums(length, view, g):
                src, dst = pool_a, pool_b
                for level in range(1, 2 * g + 3):
                    parts = slice(64, P) if level == 2 * g + 2 else slice(0, P)
                    lo, hi = 1 << (level - 1), length - (0, 0, 1, 3, 8)[level]
                    back, ahead = (1, 0) if level == 1 else (1 << (level - 2),) * 2
                    link(pool.tensor_tensor(view(dst, parts, lo, hi), view(src, parts, lo - back, hi - back),
                                            view(src, parts, lo + ahead, hi + ahead), ALU.add))
                    src, dst = dst, src

            both = ((slice(0, 64), pool_b), (slice(64, P), pool_a))
            wide = GRID_W + 2 * PAD

            def grid_rows(tensor, parts, lo, hi):
                return tensor[parts, lo * GRID_W:hi * GRID_W]

            def grid_cols(tensor, parts, lo, hi):
                return tensor[parts, 0:ROWS * wide].rearrange("p (r c) -> p r c", r=ROWS)[:, :, lo:hi]

            def line(tensor, parts, lo, hi):
                return tensor[parts, lo:hi]

            def as_grid(ap):
                return ap.rearrange("p (r c) -> p r c", r=ROWS)

            for L in range(DEPTH):
                w_last = [w for w in SWEEPS if w["layer"] == L and w["what"] == "in"][-1]
                for s in range(2):
                    pool.wait_ge(unit_done[s], w_last["base"] + w_last["n"])
                    pool.wait_ge(pair_free[s], w_last["base"] + w_last["n"])
                pool.memset(pool_w[:, :], 0.0).then_inc(poolw_zero, 1)
                pool.wait_ge(counts_full, 16 * (L + 1))
                for g in range(2):
                    link(pool.memset(pool_a[:, :], 0.0))
                    link(pool.tensor_copy(grid_rows(pool_a, slice(0, P), PAD, PAD + ROWS), tile(proj, g, SEQ)))
                    window_sums(ROWS + 2 * PAD, grid_rows, g)
                    for parts, src in both:
                        link(pool.tensor_copy(pool_c[parts, :], grid_rows(src, parts, PAD, PAD + ROWS)))
                    link(pool.memset(pool_a[:, 0:ROWS * wide], 0.0))
                    link(pool.tensor_copy(grid_cols(pool_a, slice(0, P), PAD, PAD + GRID_W), as_grid(pool_c[:, :])))
                    window_sums(wide, grid_cols, g)
                    for parts, src in both:
                        link(pool.tensor_tensor(as_grid(pool_c[parts, :]), grid_cols(src, parts, PAD, PAD + GRID_W),
                                                as_grid(pool_inv[parts, g * TOK:g * TOK + SEQ]), ALU.mult))
                    ins = pool.tensor_tensor(tile(proj, g, SEQ), pool_c[:, :], tile(proj, g, SEQ), ALU.subtract)
                    if L < DEPTH - 1:
                        link(ins)
                        link(pool.memset(pool_a[:, 0:CTX + 2 * PAD], 0.0))
                        link(pool.tensor_copy(pool_a[:, PAD:PAD + CTX], tile(proj, g, CTX, SEQ)))
                        window_sums(CTX + 2 * PAD, line, g)
                        for parts, src in both:
                            link(pool.tensor_tensor(pool_c[parts, 0:CTX], src[parts, PAD:PAD + CTX],
                                                    pool_inv[parts, g * TOK + SEQ:(g + 1) * TOK], ALU.mult))
                        ins = pool.tensor_tensor(tile(proj, g, CTX, SEQ), pool_c[:, 0:CTX], tile(proj, g, CTX, SEQ),
                                                 ALU.subtract)
                    ins.then_inc(pool_ready, 1)
                    pool.wait_ge(pool_ready, 2 * L + g + 1)


_INS = ["x", "c", "ctx", "c_ctx", "w_mod", "b_mod", "ffn1_norm", "ffn1_w1", "ffn1_w3", "ffn1_w2", "mix_norm", "w_in",
        "w_out", "pool_w", "pool_scale", "mla_q_norm", "mla_w_uq", "mla_kv_norm", "mla_w_ukv", "diff_lambda",
        "diff_subln", "ffn2_norm", "ffn2_w1", "ffn2_w3", "ffn2_w2", "final_norm"]


def rope_tables(dim):
    n_axis = dim // 4
    at = np.arange(SEQ)
    inv = (ROPE_BASE ** (-np.arange(n_axis) / n_axis)).astype(np.float32)
    ang = np.concatenate([(at // GRID_W)[:, None].astype(np.float32) * inv,
                          (at % GRID_W)[:, None].astype(np.float32) * inv], axis=-1)
    p = np.arange(P)
    cos, sin = np.cos(ang)[:, p % (dim // 2)].T, np.sin(ang)[:, p % (dim // 2)].T
    sign = np.where(p % dim < dim // 2, -1.0, 1.0)[:, None]
    swap = np.zeros((P, P), np.float32)
    swap[p ^ (dim // 2), p] = 1.0
    return cos.astype(np.float32), (sin * sign).astype(np.float32), swap


def window_counts():
    def count(n, k):
        i = np.arange(n)
        return np.clip(i + k - k // 2, 0, n) - np.clip(i - k // 2, 0, n)

    inv = np.zeros((P, 2, TOK), np.float32)
    for g, k in enumerate(WINDOWS):
        parts = slice(64 * (g % 2), 64 * (g % 2) + 64)
        inv[parts, g // 2, 0:SEQ] = 1.0 / np.outer(count(ROWS, k), count(GRID_W, k)).ravel()
        inv[parts, g // 2, SEQ:] = 1.0 / count(CTX, k)
    return inv.reshape(P, 2 * TOK)


def kernel(**inputs):
    import concourse.bacc as bacc
    from concourse.bass_utils import run_bass_kernel_spmd

    cos_d, sin_d, perm_d = rope_tables(DDIM)
    cos_m, sin_m, perm_m = rope_tables(ROPE)
    arrays = {f"in_{n}": np.ascontiguousarray(inputs[n]) for n in _INS}
    arrays.update(k_ident=np.eye(P, dtype=np.float32), k_perm_d=perm_d, k_perm_m=perm_m, k_cos_d=cos_d, k_sin_d=sin_d,
                  k_cos_m=cos_m, k_sin_m=sin_m, k_pool_inv=window_counts())
    nc = bacc.Bacc("TRN2", target_bir_lowering=False, num_devices=1)
    tensors = {n.removeprefix("in_"): nc.dram_tensor(n, a.shape, mybir.dt.from_np(a.dtype), kind="ExternalInput").ap()
               for n, a in arrays.items()}
    out = nc.dram_tensor("out", (1, SEQ, D), F32, kind="ExternalOutput").ap()
    build(nc, tensors, out)
    result = run_bass_kernel_spmd(nc, [arrays], core_ids=[0])
    return result.results[0]["out"]
```

```python
import math
from contextlib import ExitStack

import numpy as np
import concourse.bass as bass
from concourse import mybir

P = 128
D, SEQ, CTX, DEPTH = 1024, 512, 256, 2
TOK = SEQ + CTX
GRID_W = 64
ROWS = SEQ // GRID_W
N_MOD = 9
D_FF = 2816
KD = D // P
FT = D_FF // P
GROUPS = 2
FG = FT // GROUPS
HEADS = 4
NOPE, ROPE, MV = 64, 32, 64
QR, KVR = 384, 256
DDIM = 64
IN_POOL = 256
IN_MLA = QR + KVR + ROPE
EPS = 1e-6
ROPE_BASE = 10000.0
WINDOWS = (2, 4, 8, 16)
PAD = 8
UNITS_MOD = N_MOD * KD
PRO_UNITS = 2 * KD
MOD_T = 2
MOD_W = MOD_T * P
T_POOL, T_Q, T_KV, T_KR, T_DQ, T_DK, T_DV, T_IN = 0, 2, 5, 7, 8, 12, 16, 20
M_POOL, M_MLA, M_DIFF = 0, 2, 4
SC_MLA = (NOPE + ROPE) ** -0.5
SC_DIFF = DDIM ** -0.5
LAM_INIT = [0.8 - 0.6 * math.exp(-0.3 * i) for i in range(DEPTH)]
G_FFN1, G_MIX, G_FFN2, G_POOL, G_QN, G_KVN, G_SUB, G_LAYER = 0, 8, 16, 24, 26, 29, 31, 32
G_FINAL = DEPTH * G_LAYER
G_ROWS = G_FINAL + KD

F32 = mybir.dt.float32
F32R = mybir.dt.float32r
ALU = mybir.AluOpType
ACT = mybir.ActivationFunctionType
AX = mybir.AxisListType


def plan_sweeps():
    sweeps, base = [], 0

    def add(layer, what, n, kt, ctx, arg=0):
        nonlocal base
        sweeps.append(dict(layer=layer, what=what, n=n, kt=kt, ctx=ctx, arg=arg, base=base))
        base += n

    for i in range(DEPTH):
        more = i < DEPTH - 1
        for ffn in ("ffn1", "ffn2"):
            both = (ffn == "ffn1" or more,) * 2
            for g in range(GROUPS):
                add(i, ffn + "_up", FG, KD, both, g)
                add(i, ffn + "_down", KD // 2, FG, both, g)
            if ffn == "ffn1":
                add(i, "in", 2, KD, (more, more), 0)
                add(i, "in", 1, KD, (more, True), 4)
                add(i, "in", 1, KD, (True, True), 6)
                add(i, "in", 2, KD, (more, more), 8)
                add(i, "in", 4, KD, (True, True), 12)
                add(i, "out", KD // 2, KD, (more, more))
    return sweeps


def mod_tile(w):
    if w["layer"] == 0 and w["what"].startswith("ffn"):
        return PRO_UNITS + MOD_T * sum(v["n"] for v in plan_sweeps() if v["base"] < w["base"] and v["layer"] == 0
                                       and v["what"].startswith("ffn"))
    if w["layer"] == 1 and w["what"] == "ffn1_down" and w["arg"] == 0:
        return DEPTH * UNITS_MOD - MOD_T * w["n"]
    return None


def starts_norm(w):
    return w["arg"] == 0 and w["what"] in ("ffn1_up", "ffn2_up", "in")


def ends_step(w):
    return w["what"] == "out" or w["what"].endswith("_down") and w["arg"] == GROUPS - 1


def plan_groups(more):
    spans = [(0, SEQ, 0, TOK)] + ([(SEQ, CTX, SEQ, CTX)] if more else [])
    diff = [("diff", j, *s) for j in range(HEADS) for s in spans]
    mla = [("mla", 2 * m + e, *s) for m in range(HEADS // 2) for s in spans for e in range(2)]
    return diff, mla


def halves(n):
    return [(a, min(512, n - a)) for a in range(0, n, 512)]


TASKS = ([("v", a, "a") for a in range(6)] + [("rope", T_DQ + a, "d") for a in range(4)]
         + [("vm", 0, "a"), ("rope", T_DK, "d"), ("vm", 1, "a"), ("rope", T_DK + 1, "d"), ("vm", 2, "a"),
            ("rope", T_KR, "d"), ("kn", 0, "a"), ("rope", T_DK + 2, "d"), ("kn", 1, "a"), ("rope", T_DK + 3, "d"),
            ("uq", 2, "a"), ("uq", 0, "a"), ("uq", 1, "a"), ("qrope", 0, "d")])
SPLIT_AT = {("vm", 2): 0, ("kn", 0): 1, ("kn", 1): 2, ("uq", 0): 3}


def read_out(who, count):
    return sum(1 for task in TASKS[:count] if task[2] == who)


N_ACT, N_DVE = read_out("a", len(TASKS)), read_out("d", len(TASKS))
GROUPS_OF = [sum(plan_groups(i < DEPTH - 1), []) for i in range(DEPTH)]
N_DIFF = [len(plan_groups(i < DEPTH - 1)[0]) for i in range(DEPTH)]
MIX_OF = [n + 2 for n in N_DIFF]


def step_buf(L, n):
    return 2 * (n % 2) if n < sum(g[3] // P for g in GROUPS_OF[L][:N_DIFF[L]]) else n % 4


def steps_of(L):
    return [(g, gi, b) for gi, g in enumerate(GROUPS_OF[L]) for b in range(g[3] // P)]


def norm_jobs(L):
    return {n: GROUPS_OF[L][gi - N_DIFF[L]] for n, (g, gi, b) in enumerate(steps_of(L)) if g[0] == "mla" and b == 0}


N_SMALL = 4 + 7 * DEPTH
N_COUNTS = ROWS + GRID_W + CTX


def build(nc, t, out):
    SWEEPS = plan_sweeps()
    with ExitStack() as stack:
        def sb(name, cols, dt=F32, parts=P):
            return stack.enter_context(nc.sbuf_tensor(name, [parts, cols], dt))

        def sem(name):
            return stack.enter_context(nc.semaphore(name))

        def overlay(*specs):
            with ExitStack() as s:
                return [s.enter_context(nc.sbuf_tensor(n, [P, c], dt)) for n, c, dt in specs]

        x = sb("x", KD * TOK)
        raw_w = [sb(f"raw_w{s}", FG * P) for s in range(2)]
        hi_w = [sb(f"hi_w{s}", FG * P, F32R) for s in range(2)]
        lo_w = [sb(f"lo_w{s}", FG * P, F32R) for s in range(2)]
        ident = sb("ident", P)
        perm_d = sb("perm_d", P)
        perm_m = sb("perm_m", P)
        ones = sb("ones", P)
        mod = sb("mod", DEPTH * UNITS_MOD * 2)
        b_mod = sb("b_mod", DEPTH * UNITS_MOD)
        gains = sb("gains", G_ROWS)
        silu_c = sb("silu_c", KD * 2)
        scale_a = sb("scale_a", KD * 2)
        gate = sb("gate", KD * 2)
        neg_lam = sb("neg_lam", DEPTH)
        lam_sum = sb("lam_sum", 2 * DEPTH)
        lam_exp = sb("lam_exp", 2 * DEPTH)
        sub_gain = sb("sub_gain", DEPTH)
        eps_col = sb("eps_col", 1)
        pool_w = sb("pool_w_sb", 2 * P)
        half_mask = sb("half_mask", 2)
        neg_max = sb("neg_max", 8)
        exp_sum = sb("exp_sum", 8)
        inv_sum = sb("inv_sum", 8)
        cos_d = sb("cos_d", SEQ)
        sin_d = sb("sin_d", SEQ)
        rstd = sb("rstd", TOK)
        buf = [sb(f"buf{i}", TOK) for i in range(4)]
        act_buf, hid_buf, sq = buf[0], buf[1], buf[2:4]
        x_sum = buf[0]
        q_rot = buf[2]
        mod_w, mod_acc = overlay(("mod_w", KD * MOD_W, F32), ("mod_acc", 2 * MOD_W, F32))
        v_tok = sb("v_tok", (TOK // P) * 512)
        pro_w1, mod_rows = overlay(("pro_w1", KD * D, F32), ("mod_rows", 2 * D, F32))
        mla_x, wq_n, wq_r, wk_n, wk_v, pool_inv, cos_m, sin_m, pool_c, _, k_odd, pool_a, pool_b = overlay(
            ("mla_x", 2 * TOK, F32), ("wq_n", 3 * 256, F32), ("wq_r", 3 * P, F32), ("wk_n", 512, F32), ("wk_v", 512, F32),
            ("pool_inv", 2 * N_COUNTS, F32), ("cos_m", SEQ, F32), ("sin_m", SEQ, F32), ("pool_c", SEQ, F32),
            ("rest_hi", 6 * TOK - 9 * P - 1024 - 2 * N_COUNTS - 3 * SEQ, F32),
            ("k_odd", HEADS * TOK, F32), ("pool_a", 2 * TOK, F32), ("pool_b", 2 * TOK, F32))
        n_hi = sb("n_hi", KD * TOK, F32R)
        n_lo = sb("n_lo", KD * TOK, F32R)
        proj, v_mla = overlay(("proj", T_IN * TOK, F32), ("v_mla", (TOK // P) * 256, F32))
        x_tok, pro_w2, c_rows, rows, lam_row = overlay(("x_tok", (TOK // P) * D, F32), ("pro_w2", KD * D, F32),
                                               ("c_rows", P, F32),
                                               ("rows", 3 * P, F32), ("lam_row", DEPTH * 4 * DDIM, F32))
        lam_prod = sq[0]
        h_hi = sb("h_hi", FG * TOK, F32R)
        h_lo = sb("h_lo", FG * TOK, F32R)
        p_t = proj[:, T_DV * TOK:(T_DV + 2) * TOK]

        pair = [stack.enter_context(nc.psum_tensor(f"pair{i}", [P, 1024], F32)) for i in range(4)]

        raw_full = [sem(f"raw_full{s}") for s in range(2)]
        hi_ready = [sem(f"hi_ready{s}") for s in range(2)]
        lo_ready = [sem(f"lo_ready{s}") for s in range(2)]
        unit_done = [sem(f"unit_done{s}") for s in range(2)]
        pair_free = [sem(f"pair_free{s}") for s in range(2)]
        krope_full = sem("krope_full")
        c_full = sem("c_full")
        c_done = sem("c_done")
        small_full = sem("small_full")
        x_full = sem("x_full")
        pro_full = [sem("pro_full0"), sem("pro_full1")]
        cols_done = sem("cols_done")
        ones_ready = sem("ones_ready")
        cols_out = sem("cols_out")
        mrow_done = sem("mrow_done")
        mrow_out = [sem("mrow_out_act"), sem("mrow_out_dve")]
        tables_full = sem("tables_full")
        silu_ready = sem("silu_ready")
        xt_done = sem("xt_done")
        xt_out = [sem("xt_out_act"), sem("xt_out_dve")]
        lam_ready = sem("lam_ready")
        mod_full = sem("mod_full")
        mod_sum = sem("mod_sum")
        mod_done = sem("mod_done")
        mod_out = sem("mod_out")
        xsq_ready = sem("xsq_ready")
        xsum_ready = sem("xsum_ready")
        xsum_done = sem("xsum_done")
        sq_ready = sem("sq_ready")
        sq_used = sem("sq_used")
        log_ready = sem("log_ready")
        std_ready = sem("std_ready")
        applied = sem("applied")
        t_ready = sem("t_ready")
        nhi_ready = sem("nhi_ready")
        n_ready = sem("n_ready")
        hhi_ready = sem("hhi_ready")
        h_ready = sem("h_ready")
        mixw_full = sem("mixw_full")
        poolw_zero = sem("poolw_zero")
        poolw_full = sem("poolw_full")
        counts_full = sem("counts_full")
        task_done = sem("task_done")
        out_act = sem("out_act")
        out_dve = sem("out_dve")
        pool_ready = sem("pool_ready")
        pool_chain = sem("pool_chain")
        s_ready = [sem("s_ready0"), sem("s_ready1")]
        max_ready = sem("max_ready")
        exp_done = [sem("exp_done0"), sem("exp_done1")]
        p_ready = sem("p_ready")
        t_done = sem("t_done")
        pt_ready = sem("pt_ready")
        pv_done = sem("pv_done")
        o_act = sem("o_act")
        otmp_ready = sem("otmp_ready")
        k_split = sem("k_split")
        mla_hi = sem("mla_hi")
        mla_out = sem("mla_out")
        mhi_ready = sem("mhi_ready")
        mix_ready = sem("mix_ready")
        poolmm_done = sem("poolmm_done")
        fin_done = sem("fin_done")
        fin_out = sem("fin_out")
        stored = sem("stored")
        dve_chain = sem("dve_chain")

        def cols(w, i, s):
            L, what = w["layer"], w["what"]
            if what.endswith("_up"):
                src = t[what[:4] + ("_w1", "_w3")[s]][L]
                c0 = (w["arg"] * FG + i) * P
            elif what.endswith("_down"):
                src = t[what[:4] + "_w2"][L][w["arg"] * FG * P:(w["arg"] + 1) * FG * P, :]
                c0 = (2 * i + s) * P
            elif what == "in":
                src = t["w_in"][L]
                c0 = (w["arg"] + 2 * i + s) * P - (P - ROPE if w["arg"] >= T_DQ else 0)
            else:
                src, c0 = t["w_out"][L], (2 * i + s) * P
            return src.rearrange("(k p) c -> p k c", p=P)[:, :, bass.ds(c0, P)]

        def norm_width(w):
            return TOK if w["what"] == "in" else width(w, 1)

        def is_krope(w, s):
            return w["what"] == "in" and w["arg"] == 6 and s == 1

        def width(w, s):
            return TOK if w["ctx"][s] else SEQ

        def tile(tensor, k, n=TOK, at=0):
            return tensor[:, bass.ds(k * TOK + at, n)]

        def mla_q(h, n, at=0):
            return tile(proj, T_Q + h if h < 3 else T_KR, n, at)[0:NOPE + ROPE, :]

        def mla_k(h, n, at=0):
            return (tile(proj, T_KV + h, n, at) if h < 2 else tile(mla_x, h - 2, n, at))[0:NOPE + ROPE, :]

        def mod_col(L, chunk):
            return (L * UNITS_MOD + chunk * KD) * 2

        block = stack.enter_context(nc.Block())

        @block.sync
        def _(sp):
            def small(dst, src):
                sp.dma_start(dst, src).then_inc(small_full, 16)

            def as_rows(v):
                return v.rearrange("(r c) -> r c", c=P)

            sp.dma_start(c_rows[0:KD, :], as_rows(t["c"][0])).then_inc(c_full, 16)
            sp.dma_start(c_rows[KD:2 * KD, :], as_rows(t["c_ctx"])).then_inc(c_full, 16)
            sp.dma_start(ident[:, :], t["k_ident"]).then_inc(c_full, 16)
            for a in range(TOK // P):
                src = t["x"][0][a * P:(a + 1) * P, :] if a < SEQ // P else t["ctx"][0][a * P - SEQ:(a + 1) * P - SEQ, :]
                sp.dma_start(x_tok[:, a * D:(a + 1) * D], src).then_inc(x_full, 16)
            for L in range(DEPTH):
                small(rows[0:UNITS_MOD, L * P:(L + 1) * P], as_rows(t["b_mod"][L]))
                for name, col in (("ffn1_norm", G_FFN1), ("mix_norm", G_MIX), ("ffn2_norm", G_FFN2),
                                  ("pool_scale", G_POOL), ("mla_q_norm", G_QN), ("mla_kv_norm", G_KVN),
                                  ("diff_subln", G_SUB)):
                    v = as_rows(t[name][L])
                    r0 = L * G_LAYER + col
                    small(rows[r0:r0 + v.shape[0], 2 * P:3 * P], v)
            small(rows[G_FINAL:G_ROWS, 2 * P:3 * P], as_rows(t["final_norm"]))
            small(lam_row[0:1, :], t["diff_lambda"].rearrange("l a d -> (l a d)").rearrange("(o n) -> o n", o=1))
            wm = t["w_mod"][0].rearrange("(k p) c -> p k c", p=P)
            for m, dst in enumerate((pro_w1, pro_w2)):
                sp.dma_start(dst[:, :].rearrange("p (k c) -> p k c", k=KD), wm[:, :, m * D:(m + 1) * D])\
                  .then_inc(pro_full[m], 16)

            def load_unit(w, i, s, first):
                if not (first and w["base"] == 0):
                    sp.wait_ge(lo_ready[s], w["base"] + i)
                dst = raw_w[s][:, 0:w["kt"] * P].rearrange("p (k c) -> p k c", c=P)
                if is_krope(w, s):
                    src = t["w_in"][w["layer"]].rearrange("(k p) c -> p k c", p=P)[:, :, T_KR * P:T_KR * P + ROPE]
                    for r in range(HEADS):
                        sp.dma_start(dst[:, :, r * ROPE:(r + 1) * ROPE], src)\
                          .then_inc(krope_full if r else raw_full[s], 16)
                else:
                    sp.dma_start(dst, cols(w, i, s)).then_inc(raw_full[s], 16)

            def load_mod(w, i, before, L):
                if w["layer"] == 0 and w["what"] == "ffn2_up" and w["arg"] == 0 and isinstance(i, int):
                    sp.wait_ge(pv_done, len(steps_of(0)))
                if not (isinstance(before, int) and before == 0):
                    sp.wait_ge(mod_sum, 2 * KD * before)
                src = t["w_mod"][L].rearrange("(k p) c -> p k c", p=P)
                sp.dma_start(mod_w[:, :].rearrange("p (k c) -> p k c", k=KD),
                             src[:, :, bass.ds((mod_tile(w) - L * UNITS_MOD + MOD_T * i) * P, MOD_W)]).then_inc(mod_full, 16)

            batches = 0
            for q, w in enumerate(SWEEPS):
                u0 = mod_tile(w)
                if w["what"] != "out":
                    load_unit(w, 0, 0, True)
                    load_unit(w, 0, 1, True)
                if u0 is not None:
                    load_mod(w, 0, batches, 0 if u0 < UNITS_MOD else 1)
                cut = (UNITS_MOD - u0) // MOD_T if u0 is not None and u0 < UNITS_MOD < u0 + MOD_T * w["n"] else w["n"]
                for a, b in ((1, cut), (cut, w["n"])):
                    if a < b:
                        with sp.Fori(a, b) as i:
                            load_unit(w, i, 0, False)
                            load_unit(w, i, 1, False)
                            if u0 is not None:
                                load_mod(w, i, batches + i, int(u0 + MOD_T * a >= UNITS_MOD))
                if q == 0:
                    for dst, name in ((perm_d, "k_perm_d"), (perm_m, "k_perm_m"), (cos_d, "k_cos_d"), (sin_d, "k_sin_d")):
                        sp.dma_start(dst[:, :], t[name]).then_inc(tables_full, 16)
                if u0 is not None:
                    batches += w["n"]
                if w["what"] == "in" and w["arg"] == 12:
                    L = w["layer"]
                    load_unit(SWEEPS[q + 1], 0, 0, True)
                    load_unit(SWEEPS[q + 1], 0, 1, True)
                    for s in range(2):
                        sp.wait_ge(unit_done[s], w["base"] + w["n"])
                    uq = t["mla_w_uq"][L].rearrange("(k p) (h c) -> p k h c", p=P, h=HEADS)
                    ukv = t["mla_w_ukv"][L].rearrange("(k p) (h c) -> p k h c", p=P, h=HEADS)
                    for k in range(QR // P):
                        sp.dma_start(wq_n[:, k * 256:(k + 1) * 256].rearrange("p (h c) -> p h c", h=HEADS),
                                     uq[:, k, :, 0:NOPE]).then_inc(mixw_full, 16)
                        sp.dma_start(wq_r[:, k * P:(k + 1) * P].rearrange("p (h c) -> p h c", h=HEADS),
                                     uq[:, k, :, NOPE:NOPE + ROPE]).then_inc(mixw_full, 16)
                    for k in range(KVR // P):
                        sp.dma_start(wk_n[:, k * 256:(k + 1) * 256].rearrange("p (h c) -> p h c", h=HEADS),
                                     ukv[:, k, :, 0:NOPE]).then_inc(mixw_full, 16)
                        sp.dma_start(wk_v[:, k * 256:(k + 1) * 256].rearrange("p (h c) -> p h c", h=HEADS),
                                     ukv[:, k, :, NOPE:NOPE + MV]).then_inc(mixw_full, 16)
                    sp.dma_start(cos_m[:, :], t["k_cos_m"]).then_inc(mixw_full, 16)
                    sp.dma_start(sin_m[:, :], t["k_sin_m"]).then_inc(mixw_full, 16)
                    sp.dma_start(pool_inv[:, :], t["k_pool_inv"]).then_inc(counts_full, 16)
                    sp.wait_ge(poolw_zero, L + 1)
                    for g in range(len(WINDOWS)):
                        e = 64 * (g % 2)
                        sp.dma_start(pool_w[e:e + 64, (g // 2) * P + e:(g // 2) * P + e + 64],
                                     t["pool_w"][L][g]).then_inc(poolw_full, 16)
            for a in range(SEQ // P):
                sp.wait_ge(fin_out, a + 1)
                sp.dma_start(out[0][a * P:(a + 1) * P, :], x_tok[:, a * D:(a + 1) * D]).then_inc(stored, 16)
            sp.wait_ge(stored, 16 * (SEQ // P))

        @block.tensor
        def _(pe):
            pe.wait_ge(c_full, 16 * 3)
            pe.transpose(pair[2][:, 0:2 * KD], c_rows[0:2 * KD, :], ident[0:2 * KD, 0:2 * KD]).then_inc(c_done, 1)
            for k in range(KD):
                if k == 0:
                    pe.wait_ge(x_full, 16 * (TOK // P))
                if k >= 2:
                    pe.wait_ge(xt_out[k % 2], k // 2)
                for a in range(TOK // P):
                    mm = pe.transpose(pair[k % 2][:, a * P:(a + 1) * P], x_tok[:, a * D + k * P:a * D + (k + 1) * P],
                                      ident[:, :])
                mm.then_inc(xt_done, 1)
            pe.wait_ge(small_full, 16 * N_SMALL)
            pe.wait_ge(ones_ready, 1)
            for L in range(DEPTH):
                pe.transpose(pair[3][:, L * P:L * P + UNITS_MOD], rows[0:UNITS_MOD, L * P:(L + 1) * P],
                             ident[0:UNITS_MOD, 0:UNITS_MOD])
            pe.transpose(pair[3][:, 2 * P:2 * P + G_ROWS], rows[0:G_ROWS, 2 * P:3 * P], ident[0:G_ROWS, 0:G_ROWS])
            pe.matmul(pair[3][:, 512:1024], ones[0:1, :], lam_row[0:1, :], start=True, stop=True).then_inc(cols_done, 1)

            def first_mod(m, src):
                pe.wait_ge(silu_ready, 2)
                pe.wait_ge(pro_full[m], 16)
                for a in range(0, D, 512):
                    for k in range(KD):
                        mm = pe.matmul(pair[m][0:2, a:a + 512], silu_c[:, 2 * k:2 * k + 2],
                                       src[:, k * D + a:k * D + a + 512], start=(k == 0), stop=(k == KD - 1))
                mm.then_inc(mrow_done, 1)

            def mod_columns():
                for m in range(2):
                    pe.wait_ge(mrow_out[m], 1)
                    for u in range(m * KD, (m + 1) * KD):
                        mm = pe.transpose(pair[2][:, 2 * u:2 * u + 2], mod_rows[0:2, u * P:(u + 1) * P], ident[0:2, 0:2])
                mm.then_inc(mod_done, 1)

            cnt = dict(x=0, sq=0, std=0, batch=1, n=0, h=0, s=[0, 0], step=0, oact=0, mix=0)

            def sum_stream(w_cols):
                cnt["x"] += 1
                if cnt["std"]:
                    pe.wait_ge(std_ready, cnt["std"])
                pe.wait_ge(xsum_ready, KD * cnt["x"])
                for a, m in halves(w_cols):
                    pe.matmul(pair[3][:, a:a + m], ones[:, :], x_sum[:, a:a + m], start=True, stop=False)
                pe.wait_ge(xsq_ready, KD * cnt["x"])
                for a, m in halves(w_cols):
                    mm = pe.matmul(pair[3][:, a:a + m], ones[:, :], sq[1][:, a:a + m], start=False, stop=True)
                mm.then_inc(xsum_done, 1)
                cnt["std"] += 1

            def sum_squares(n_tiles, w_cols, dst):
                if cnt["std"]:
                    pe.wait_ge(std_ready, cnt["std"])
                for k in range(n_tiles):
                    pe.wait_ge(sq_ready, cnt["sq"] + 1)
                    for a, m in halves(w_cols):
                        mm = pe.matmul(dst[:, a:a + m], ones[:, :], sq_src(cnt["sq"])[:, a:a + m],
                                       start=(k == 0), stop=(k == n_tiles - 1))
                    mm.then_inc(sq_used, 1)
                    cnt["sq"] += 1
                cnt["std"] += 1

            def sq_src(n):
                return sq[n % 2]

            def unit(w, i, slots, first):
                down = w["what"].endswith("_down")
                src_hi, src_lo = (h_hi, h_lo) if down else (n_hi, n_lo)
                for s in slots:
                    pe.wait_ge(lo_ready[s], w["base"] + i + 1)
                    if not (first and w["base"] == 0):
                        pe.wait_ge(pair_free[s], w["base"] + i)
                order = [*range(M_MLA, KD), *range(M_MLA)] if w["what"] == "out" else range(w["kt"])
                for n, k in enumerate(order):
                    if down:
                        pe.wait_ge(h_ready, cnt["h"] + k + 1)
                    elif w["what"] == "out":
                        if k >= M_DIFF or k < M_MLA:
                            late = (KD - 1 - k) * N_DIFF[w["layer"]] // HEADS + 2 if k >= M_DIFF else 1 - k
                            pe.wait_ge(mix_ready, cnt["mix"] - late)
                    else:
                        pe.wait_ge(n_ready, cnt["n"] + k + 1)
                    for s in slots:
                        hi, lo = hi_w[s], lo_w[s]
                        for wt, src in ((hi, src_hi), (hi, src_lo), (lo, src_hi)):
                            for a, m in halves(width(w, s)):
                                mm = pe.matmul(pair[s][:, a:a + m], wt[:, k * P:(k + 1) * P], tile(src, k, m, a),
                                               start=(n == 0 and wt is hi and src is src_hi),
                                               stop=(n == w["kt"] - 1 and wt is lo))
                        if n == w["kt"] - 1:
                            mm.then_inc(unit_done[s], 1)

            def mod_tiles(w, i):
                b = cnt["batch"] + i
                pe.wait_ge(mod_sum, 2 * KD * b)
                pe.wait_ge(mod_out, b)
                for m in range(MOD_T):
                    for e in range(2):
                        mm = pe.matmul(pair[2][:, (2 * m + e) * P:(2 * m + e + 1) * P],
                                       mod_acc[:, e * MOD_W + m * P:e * MOD_W + (m + 1) * P], ones[:, :],
                                       start=True, stop=True)
                mm.then_inc(mod_done, 1)

            def sweep(w):
                per = mod_tile(w) is not None
                if starts_norm(w):
                    unit(w, 0, (0, 1), True)
                else:
                    unit(w, 0, (0,), True)
                    unit(w, 0, (1,), True)
                if per:
                    mod_tiles(w, 0)
                if w["n"] > 1:
                    with pe.Fori(1, w["n"]) as i:
                        unit(w, i, (0,), False)
                        unit(w, i, (1,), False)
                        if per:
                            mod_tiles(w, i)
                if per:
                    cnt["batch"] += w["n"]

            def mixer(L):
                w_last = [w for w in SWEEPS if w["layer"] == L and w["what"] == "in"][-1]
                more = L < DEPTH - 1
                nq_all = TOK if more else SEQ
                for s in range(2):
                    pe.wait_ge(pair_free[s], w_last["base"] + w_last["n"])
                pe.wait_ge(mod_out, cnt["batch"])

                def task_start(a):
                    if a >= 3:
                        who = TASKS[a - 3][2]
                        freed, each = (out_act, N_ACT) if who == "a" else (out_dve, N_DVE)
                        pe.wait_ge(freed, L * each + read_out(who, a - 2))
                    return pair[a % 3]

                for a, (what, arg, _) in enumerate(TASKS):
                    if a == 2:
                        sum_squares(2, TOK, pair[3])
                    if a == 5:
                        sum_squares(3, nq_all, pair[3])
                    if what == "vm" and arg == 0:
                        pe.wait_ge(mixw_full, 16 * 12 * (L + 1))
                        pe.wait_ge(applied, 2 * L + 1)
                    if what == "uq" and arg == 2:
                        pe.wait_ge(applied, 2 * L + 2)
                    if what == "rope" and arg == T_DQ:
                        pe.wait_ge(tables_full, 16 * 4)
                    if what == "qrope":
                        pe.wait_ge(out_act, L * N_ACT + read_out("a", TASKS.index(("uq", 2, "a")) + 1))
                    dst = task_start(a)
                    if what == "v":
                        for j in range(HEADS):
                            mm = pe.transpose(dst[:, j * P:(j + 1) * P], tile(proj, T_DV + j, P, arg * P), ident[:, :])
                    elif what == "rope":
                        perm = perm_d if T_DQ <= arg < T_DV else perm_m
                        mm = pe.matmul(dst[:, 0:SEQ], perm[:, :], tile(proj, arg, SEQ), start=True, stop=True)
                    elif what == "qrope":
                        mm = pe.matmul(dst[:, 0:SEQ], perm_m[:, :], q_rot[:, 0:SEQ], start=True, stop=True)
                    elif what == "vm":
                        for e in range(2):
                            for k in range(2):
                                mm = pe.matmul(dst[:, e * 512:e * 512 + 256], tile(proj, T_KV + k, P, (2 * arg + e) * P),
                                               wk_v[:, k * 256:(k + 1) * 256], start=(k == 0), stop=(k == 1))
                    elif what == "kn":
                        for b, m in halves(TOK):
                            for k in range(2):
                                mm = pe.matmul(dst[:, b:b + m], wk_n[:, k * 256 + arg * P:k * 256 + (arg + 1) * P],
                                               tile(proj, T_KV + k, m, b), start=(k == 0), stop=(k == 1))
                    else:
                        for b, m in halves(nq_all):
                            for k in range(3):
                                lhs = (wq_n[:, k * 256 + arg * P:k * 256 + (arg + 1) * P] if arg < 2
                                       else wq_r[:, k * P:(k + 1) * P])
                                mm = pe.matmul(dst[:, b:b + m], lhs, tile(proj, T_Q + k, m, b),
                                               start=(k == 0), stop=(k == 2))
                    mm.then_inc(task_done, 1)
                pe.wait_ge(out_act, (L + 1) * N_ACT)
                pe.wait_ge(out_dve, (L + 1) * N_DVE - 1)
                pe.wait_ge(std_ready, cnt["std"])

                steps = steps_of(L)

                def scores(n, kind, h, q0, k0, nk, s):
                    if cnt["s"][s]:
                        pe.wait_ge(exp_done[s], cnt["s"][s])
                    if kind == "diff":
                        pe.wait_ge(k_split, 2 * (L * HEADS + h + 1))
                    for a, m in halves(nk):
                        if kind == "diff":
                            mm = pe.matmul(pair[s][:, a:a + m], tile(proj, T_DQ + h, P, q0),
                                           tile(k_odd, h, m, k0 + a) if s else tile(proj, T_DK + h, m, k0 + a),
                                           start=True, stop=True)
                        else:
                            mm = pe.matmul(pair[s][:, a:a + m], mla_q(h, P, q0), mla_k(h, m, k0 + a),
                                           start=True, stop=True)
                    mm.then_inc(s_ready[s], 1)
                    cnt["s"][s] += 1

                st0 = cnt["step"]
                def transposes(m):
                    if not 0 <= m < len(steps):
                        return
                    if m == 0:
                        pe.wait_ge(out_dve, (L + 1) * N_DVE)
                    nk, src = steps[m][0][5], buf[step_buf(L, m)]
                    pe.wait_ge(p_ready, st0 + m + 1)
                    if st0 + m:
                        pe.wait_ge(pt_ready, st0 + m)
                    for a in range(nk // P):
                        mm = pe.transpose(pair[2][:, a * P:(a + 1) * P], src[:, a * P:(a + 1) * P], ident[:, :])
                    mm.then_inc(t_done, 1)

                jobs = norm_jobs(L)
                for n in range(len(steps) + 3):
                    if n < len(steps):
                        (kind, h, q0, nq, k0, nk), gi, b = steps[n]
                        if kind == "diff":
                            scores(n, kind, h, q0 + b * P, k0, nk, 0)
                            scores(n, kind, h, q0 + b * P, k0, nk, 1)
                            transposes(n - 2)
                        else:
                            scores(n, kind, h, q0 + b * P, k0, nk, n % 2)
                            transposes(n - 2)
                    else:
                        transposes(n - 2)
                    if n < 2:
                        continue
                    m = n - 2
                    if m - 1 in jobs:
                        dn = jobs[m - 1][3]
                        pe.wait_ge(std_ready, cnt["std"])
                        pe.wait_ge(sq_ready, cnt["sq"] + 1)
                        pe.matmul(pair[3][:, 512:512 + dn], ones[:, :], tile(proj, T_DK, dn),
                                  start=True, stop=True).then_inc(sq_used, 1)
                        cnt["sq"] += 1
                        cnt["std"] += 1
                    if n < 3:
                        continue
                    m = n - 3
                    (kind, h, q0, nq, k0, nk), gi, b = steps[m]
                    pe.wait_ge(pt_ready, st0 + m + 1)
                    if b == 0:
                        e = gi - N_DIFF[L]
                        if e <= 0 and cnt["oact"]:
                            pe.wait_ge(o_act, cnt["oact"])
                        if kind == "diff":
                            cnt["oact"] += 1
                        elif e and e % 2 == 0:
                            pe.wait_ge(mla_out, (sum(N_DIFF[:L]) + e) // 2)
                    for a in range(nk // P):
                        kt = k0 // P + a
                        e = 64 * (h % 2)
                        if kind == "diff":
                            dst, v = pair[3][:, b * P:(b + 1) * P], v_tok[:, kt * 512 + h * P:kt * 512 + (h + 1) * P]
                        else:
                            dst = pair[3][e:e + 64, b * P:(b + 1) * P]
                            v = v_mla[:, kt * 256 + h * MV:kt * 256 + (h + 1) * MV]
                        mm = pe.matmul(dst, v, tile(p_t, m % 2, P, a * P), start=(a == 0), stop=(a == nk // P - 1))
                    mm.then_inc(pv_done, 1)
                cnt["step"] += len(steps)
                pe.wait_ge(pool_ready, 2 * (L + 1))
                pe.wait_ge(poolw_full, 16 * len(WINDOWS) * (L + 1))
                pe.wait_ge(pt_ready, cnt["step"])
                pe.wait_ge(std_ready, cnt["std"])
                pe.wait_ge(mla_out, sum(N_DIFF[:L + 1]) // 2)
                for a in range(2):
                    for b, m in halves(nq_all):
                        mm = pe.matmul(pair[2 + a][:, b:b + m], pool_w[:, a * P:(a + 1) * P], tile(proj, T_POOL + a, m, b),
                                       start=True, stop=True)
                    mm.then_inc(poolmm_done, 1)
                for a in range(2):
                    pe.wait_ge(exp_done[a], cnt["s"][a])
                cnt["mix"] = sum(MIX_OF[:L + 1])

            for q, w in enumerate(SWEEPS):
                if starts_norm(w):
                    if q == 0:
                        for e in range(2):
                            pe.wait_ge(xt_out[e], KD // 2)
                        pe.wait_ge(cols_out, 1)
                        first_mod(0, pro_w1)
                    sum_stream(norm_width(w))
                    if q == 0:
                        first_mod(1, pro_w2)
                        mod_columns()
                if w["what"] == "out":
                    mixer(w["layer"])
                sweep(w)
                if w["what"] == "in" and w["arg"] == 12 or w["what"].endswith("_up") and w["arg"] == 1:
                    cnt["n"] += KD
                if w["what"].endswith("_down"):
                    cnt["h"] += FG
            sum_stream(SEQ)
            pe.wait_ge(n_ready, cnt["n"] + KD)
            for a in range(SEQ // P):
                if a < 2:
                    pe.wait_ge(pair_free[a], SWEEPS[-1]["base"] + SWEEPS[-1]["n"])
                else:
                    pe.wait_ge(fin_out, a - 1)
                for k in range(KD):
                    mm = pe.transpose(pair[a % 2][:, k * P:(k + 1) * P], tile(x, k, P, a * P), ident[:, :])
                mm.then_inc(fin_done, 1)

        @block.scalar
        def _(act):
            act.wait_ge(c_done, 1)
            for e in range(2):
                act.activation(silu_c[:, e:2 * KD:2], pair[2][:, e * KD:(e + 1) * KD], ACT.Silu).then_inc(silu_ready, 1)
            for k in range(0, KD, 2):
                act.wait_ge(xt_done, k + 1)
                act.copy(tile(x, k), pair[0][:, 0:TOK]).then_inc(xt_out[0], 1)
            act.wait_ge(lam_ready, 1)
            act.activation(lam_exp[:, :], lam_sum[:, :], ACT.Exp).then_inc(lam_ready, 1)

            cnt = dict(x=0, sq=0, std=0, used=None, n=0, step=0, s=0, otmp=0, dhi=0)

            def split_hi(w, i, s, first):
                act.wait_ge(raw_full[s], (w["base"] + i + 1) * 16)
                if is_krope(w, s):
                    act.wait_ge(krope_full, 16 * (HEADS - 1) * (w["layer"] + 1))
                if not (first and w["base"] == 0):
                    act.wait_ge(unit_done[s], w["base"] + i)
                act.copy(hi_w[s][:, 0:w["kt"] * P], raw_w[s][:, 0:w["kt"] * P]).then_inc(hi_ready[s], 1)

            def square(src, w_cols, dst=None):
                if cnt["sq"] >= 2:
                    act.wait_ge(sq_used, cnt["sq"] - 1)
                act.activation((sq[cnt["sq"] % 2] if dst is None else dst)[:, 0:w_cols], src, ACT.Square)\
                   .then_inc(sq_ready, 1)
                cnt["sq"] += 1

            def square_x(i, s, w_cols):
                act.wait_ge(xsum_ready, KD * cnt["x"] + 2 * i + s)
                act.activation(sq[s][:, 0:w_cols], tile(x, 2 * i + s, w_cols), ACT.Square).then_inc(xsq_ready, 1)

            def std(src, w_cols, n):
                if cnt["used"]:
                    act.wait_ge(*cnt["used"])
                cnt["std"] += 1
                act.activation(rstd[:, 0:w_cols], src[:, 0:w_cols], ACT.Ln, bias=eps_col[:, 0:1], scale=1.0 / n)\
                   .then_inc(log_ready, 1)
                act.wait_ge(log_ready, cnt["std"])
                act.activation(rstd[:, 0:w_cols], rstd[:, 0:w_cols], ACT.Exp, scale=-0.5).then_inc(std_ready, 1)

            def norm_x(w_cols, w, shift):
                if w is not None:
                    split_hi(w, 0, 1, True)
                cnt["x"] += 1
                act.wait_ge(xsum_done, cnt["x"])
                std(pair[3], w_cols, D)
                if shift is None:
                    return
                if cnt["n"] == 0:
                    act.wait_ge(mrow_done, 1)
                    act.copy(mod_rows[0:2, 0:D], pair[0][0:2, :]).then_inc(mrow_out[0], 1)
                for k in range(KD):
                    act.wait_ge(t_ready, cnt["n"] + k + 1)
                    for e, (a, m) in enumerate(halves(w_cols)):
                        ins = act.activation(tile(n_hi, k, m, a), buf[k % 2][:, a:a + m], ACT.Identity,
                                             bias=mod[:, shift + 2 * k + e:shift + 2 * k + e + 1])
                    ins.then_inc(nhi_ready, 1)
                cnt["n"] += KD
                cnt["used"] = (t_ready, cnt["n"])

            def finish(w, i, s):
                n, what = w["base"] + i + 1, w["what"]
                if what.endswith("_up"):
                    if s == 0:
                        act.wait_ge(unit_done[0], n)
                        if not (isinstance(n, int) and n == 1):
                            act.wait_ge(pair_free[1], n - 1)
                        act.activation(act_buf[:, 0:width(w, 0)], pair[0][:, 0:width(w, 0)], ACT.Silu)\
                           .then_inc(pair_free[0], 1)
                    else:
                        act.wait_ge(pair_free[1], n)
                        act.copy(tile(h_hi, i, width(w, 1)), hid_buf[:, 0:width(w, 1)]).then_inc(hhi_ready, 1)
                elif ends_step(w):
                    act.wait_ge(pair_free[s], n)
                    square_x(i, s, width(w, s))
                elif what == "in" and s == 0:
                    act.wait_ge(unit_done[0], n)
                    act.activation(tile(proj, w["arg"] + 2 * i, width(w, 0)), pair[0][:, 0:width(w, 0)], ACT.Identity,
                                   scale=SC_DIFF if w["arg"] == T_DQ else 1.0).then_inc(pair_free[0], 1)

            def sweep(q):
                w = SWEEPS[q]
                if not starts_norm(w):
                    split_hi(w, 0, 1, True)
                finish(w, 0, 0)
                if w["n"] > 1:
                    with act.Fori(1, w["n"]) as i:
                        split_hi(w, i, 0, False)
                        finish(w, i - 1, 1)
                        split_hi(w, i, 1, False)
                        finish(w, i, 0)
                if q + 1 < len(SWEEPS):
                    split_hi(SWEEPS[q + 1], 0, 0, True)
                finish(w, w["n"] - 1, 1)

            def mixer(L):
                w_last = [w for w in SWEEPS if w["layer"] == L and w["what"] == "in"][-1]
                more = L < DEPTH - 1
                nq_all = TOK if more else SEQ
                act.wait_ge(pair_free[1], w_last["base"] + w_last["n"])
                act.wait_ge(pair_free[0], w_last["base"] + w_last["n"])
                for k in range(2):
                    square(tile(proj, T_KV + k), TOK)
                for a, (what, arg, who) in enumerate(TASKS):
                    if a == 2:
                        act.wait_ge(sq_used, cnt["sq"])
                        std(pair[3], TOK, KVR)
                        cnt["used"] = (applied, 2 * L + 1)
                    if a == 3:
                        for k in range(3):
                            square(tile(proj, T_Q + k, nq_all), nq_all)
                    if a == 6:
                        act.wait_ge(sq_used, cnt["sq"])
                        std(pair[3], nq_all, QR)
                        cnt["used"] = (applied, 2 * L + 2)
                    if who != "a":
                        continue
                    if (what, arg) in SPLIT_AT:
                        j = SPLIT_AT[what, arg]
                        act.wait_ge(out_dve, L * N_DVE + read_out("d", TASKS.index(("rope", T_DK + j, "d")) + 1))
                        for e, dst in enumerate((tile(k_odd, j), tile(proj, T_DK + j))):
                            if e:
                                act.wait_ge(k_split, 2 * (L * HEADS + j) + 1)
                            act.activation(dst, tile(proj, T_DK + j), ACT.Identity, scale=half_mask[:, 1 - e:2 - e])\
                               .then_inc(k_split, 1)
                    last = {"kn": 1, "uq": 1}.get(what, arg) if arg < 2 else arg
                    act.wait_ge(task_done, L * len(TASKS) + TASKS.index((what, last, who)) + 1)
                    src = pair[a % 3]
                    if what == "v":
                        ins = act.copy(v_tok[:, arg * 512:(arg + 1) * 512], src[:, 0:512])
                    elif what == "vm":
                        ins = act.copy(v_mla[:, arg * 512:(arg + 1) * 512].rearrange("p (e c) -> p e c", e=2),
                                       src[:, :].rearrange("p (e c) -> p e c", e=2)[:, :, 0:256])
                    elif what == "uq" and arg == 2:
                        ins = act.activation(q_rot[:, 0:nq_all], src[:, 0:nq_all], ACT.Identity, scale=SC_MLA)
                    else:
                        if what == "uq" and arg == 1:
                            act.wait_ge(out_dve, L * N_DVE + read_out("d", TASKS.index(("rope", T_KR, "d")) + 1))
                        of, m = (mla_k, TOK) if what == "kn" else (mla_q, nq_all)
                        for e in range(2):
                            ins = act.activation(of(2 * arg + e, m)[0:NOPE, :], src[NOPE * e:NOPE * (e + 1), 0:m],
                                                 ACT.Identity, scale=SC_MLA if what == "uq" else 1.0)
                    ins.then_inc(out_act, 1)
                steps = steps_of(L)
                st0 = cnt["step"]
                jobs = norm_jobs(L)
                for n in range(len(steps) + 5):
                    if n < len(steps):
                        (kind, h, q0, nq, k0, nk), gi, b = steps[n]
                        if n >= min(jobs) + 4:
                            act.wait_ge(t_done, st0 + n - 3)
                        elif n >= 2:
                            act.wait_ge(t_done, st0 + n - 1)
                        else:
                            act.wait_ge(out_dve, (L + 1) * N_DVE)
                        for s in ((0, 1) if kind == "diff" else (n % 2,)):
                            c = cnt["s"]
                            act.wait_ge(max_ready, c + 1)
                            act.activation(buf[step_buf(L, n) + (s if kind == "diff" else 0)][:, 0:nk], pair[s][:, 0:nk],
                                           ACT.Exp, bias=neg_max[:, c % 8:c % 8 + 1],
                                           accum_out=exp_sum[:, c % 8:c % 8 + 1]).then_inc(exp_done[s], 1)
                            cnt["s"] += 1
                    if n < 2:
                        continue
                    m = n - 2
                    if m < len(steps):
                        (kind, h, q0, nq, k0, nk), gi, b = steps[m]
                        act.wait_ge(t_done, st0 + m + 1)
                        if m >= 2:
                            act.wait_ge(pv_done, st0 + m - 1)
                        act.copy(tile(p_t, m % 2, nk), pair[2][:, 0:nk]).then_inc(pt_ready, 1)
                    if m in jobs:
                        if m == min(jobs):
                            act.wait_ge(o_act, len(jobs) - 1 + sum(N_DIFF[:L]))
                        _, dh, dq, dn, _, _ = jobs[m]
                        square(tile(proj, T_DQ + dh, dn, dq), dn, tile(proj, T_DK, dn))
                    if m - 1 in jobs:
                        act.wait_ge(sq_used, cnt["sq"])
                        std(pair[3][:, 512:1024], jobs[m - 1][3], 2 * DDIM)
                        cnt["otmp"] += 1
                        cnt["used"] = (otmp_ready, cnt["otmp"])
                    if m - 3 in jobs:
                        if m - 3 == min(jobs):
                            act.wait_ge(pool_ready, 2 * (L + 1))
                        _, dh, dq, dn, _, _ = jobs[m - 3]
                        cnt["dhi"] += 1
                        act.wait_ge(otmp_ready, cnt["dhi"])
                        act.copy(tile(n_hi, M_DIFF + dh, dn, dq), tile(proj, T_DK + 1, dn)).then_inc(mhi_ready, 1)
                    m = n - 3
                    if not 0 <= m < len(steps):
                        continue
                    (kind, h, q0, nq, k0, nk), gi, b = steps[m]
                    if b < nq // P - 1:
                        continue
                    if kind == "diff":
                        act.wait_ge(pv_done, st0 + m + 1)
                        act.copy(tile(proj, T_DQ + h, nq, q0), pair[3][:, 0:nq]).then_inc(o_act, 1)
                    elif h % 2:
                        act.wait_ge(pv_done, st0 + m + 1)
                        act.copy(tile(n_hi, M_MLA + h // 2, nq, q0), pair[3][:, 0:nq]).then_inc(mla_hi, 1)
                cnt["step"] += len(steps)
                for a in range(2):
                    act.wait_ge(poolmm_done, 2 * L + a + 1)
                    g = L * G_LAYER + G_POOL + a
                    act.activation(tile(n_hi, M_POOL + a, nq_all), pair[2 + a][:, 0:nq_all], ACT.Identity,
                                   scale=gains[:, g:g + 1]).then_inc(mhi_ready, 1)

            act.wait_ge(cols_out, 1)
            for q, w in enumerate(SWEEPS):
                if starts_norm(w):
                    chunk = {"ffn1_up": 0, "in": 3, "ffn2_up": 6}[w["what"]]

                    if q == 0:
                        for k in range(KD):
                            act.wait_ge(xt_out[k % 2], k // 2 + 1)
                            square_x(k // 2, k % 2, TOK)
                        split_hi(w, 0, 0, True)
                    norm_x(norm_width(w), w, mod_col(w["layer"], chunk))
                if w["what"] == "out":
                    mixer(w["layer"])
                sweep(q)
            norm_x(SEQ, None, None)
            for a in range(0, SEQ // P):
                act.wait_ge(fin_done, a + 1)
                act.copy(x_tok[:, a * D:(a + 1) * D], pair[a % 2][:, :]).then_inc(fin_out, 1)

        @block.vector
        def _(dve):
            links = 0

            def link(ins):
                nonlocal links
                links += 1
                ins.then_inc(dve_chain, 1)
                dve.wait_ge(dve_chain, links)

            dve.memset(eps_col[:, :], EPS)
            link(dve.memset(half_mask[:, :], 0.0))
            for e in range(2):
                dve.memset(half_mask[e * DDIM:(e + 1) * DDIM, e:e + 1], 1.0)
            dve.memset(ones[:, :], 1.0).then_inc(ones_ready, 1)
            dve.memset(x_sum[:, :], 0.0).then_inc(xsum_ready, 1)
            for k in range(1, KD, 2):
                dve.wait_ge(xt_done, k + 1)
                dve.tensor_copy(tile(x, k), pair[1][:, 0:TOK]).then_inc(xt_out[1], 1)
            dve.wait_ge(cols_done, 1)
            dve.tensor_copy(b_mod[:, 0:UNITS_MOD], pair[3][:, 0:UNITS_MOD])
            dve.tensor_copy(b_mod[:, UNITS_MOD:], pair[3][:, P:P + UNITS_MOD])
            dve.tensor_copy(gains[:, :], pair[3][:, 2 * P:2 * P + G_ROWS])
            link(dve.tensor_copy(lam_prod[:, 0:512], pair[3][:, 512:1024]))
            lv = lam_prod[:, 0:512].rearrange("p (l two d) -> p l two d", two=2, d=DDIM)
            products = lam_prod[:, 512:768].rearrange("p (l d) -> p l d", d=DDIM)
            dve.tensor_tensor(products, lv[:, :, 0, :], lv[:, :, 1, :], ALU.mult).then_inc(cols_out, 1)
            dve.wait_ge(cols_out, 1)
            dve.tensor_reduce(lam_sum[:, :], products, AX.X, ALU.add).then_inc(lam_ready, 1)
            dve.wait_ge(lam_ready, 2)
            for L in range(DEPTH):
                link(dve.tensor_tensor(neg_lam[:, L:L + 1], lam_exp[:, 2 * L + 1:2 * L + 2], lam_exp[:, 2 * L:2 * L + 1],
                                       ALU.subtract))
                link(dve.tensor_scalar(neg_lam[:, L:L + 1], neg_lam[:, L:L + 1], -LAM_INIT[L], None, ALU.add))
                g = L * G_LAYER + G_SUB
                link(dve.tensor_scalar(sub_gain[:, L:L + 1], gains[:, g:g + 1], 1.0 - LAM_INIT[L], None, ALU.mult))
            cnt = dict(x=0, std=0, n=0, h=0, batch=1, s=0, sp=[0, 0], ex=[0, 0], mhi=0, mix=0, mla=0)

            def split_lo(w, i, s):
                dve.wait_ge(hi_ready[s], w["base"] + i + 1)
                m = w["kt"] * P
                dve.tensor_tensor(lo_w[s][:, 0:m], raw_w[s][:, 0:m], hi_w[s][:, 0:m].bitcast(F32), ALU.subtract)\
                   .then_inc(lo_ready[s], 1)

            def clear_x():
                dve.memset(x_sum[:, :], 0.0).then_inc(xsum_ready, 1)

            def add_x(i, s, w_cols):
                dve.wait_ge(xsq_ready, KD * cnt["x"] + 2 * i + s + 1)
                dve.wait_ge(xsum_ready, KD * cnt["x"] + 2 * i + s + 1)
                dve.tensor_tensor(x_sum[:, 0:w_cols], x_sum[:, 0:w_cols], sq[s][:, 0:w_cols], ALU.add)\
                   .then_inc(xsum_ready, 1)

            def wait_rstd():
                dve.wait_ge(std_ready, cnt["std"] + 1)
                cnt["std"] += 1

            def norm_x(w, w_cols, L, gain, shift):
                parts = list(enumerate(halves(w_cols)))
                if cnt["n"] == 0:
                    for k in range(KD - 1):
                        add_x(k // 2, k % 2, TOK)
                    split_lo(w, 0, 0)
                    dve.wait_ge(mrow_done, 2)
                    dve.tensor_copy(mod_rows[0:2, D:2 * D], pair[1][0:2, :]).then_inc(mrow_out[1], 1)
                    dve.wait_ge(mod_done, 1)
                    for e in range(2):
                        ins = dve.tensor_tensor(mod[:, e:2 * PRO_UNITS:2], pair[2][:, e:2 * PRO_UNITS:2],
                                                b_mod[:, 0:PRO_UNITS], ALU.add)
                    ins.then_inc(mod_out, 1)
                dve.wait_ge(mod_out, cnt["batch"])
                for e in range(2):
                    ins = dve.scalar_tensor_tensor(out=scale_a[:, e:16:2], in0=mod[:, shift + 16 + e:shift + 32:2], scalar=1.0,
                                                   in1=gains[:, gain:gain + KD], op0=ALU.add, op1=ALU.mult)
                link(ins)
                cnt["x"] += 1
                split_lo(w, 0, 1)
                wait_rstd()

                def low(k):
                    dve.wait_ge(nhi_ready, cnt["n"] + k + 1)
                    for e, (a, m) in parts:
                        ins = dve.scalar_tensor_tensor(out=tile(n_lo, k, m, a), in0=buf[k % 2][:, a:a + m],
                                                       scalar=mod[:, shift + 2 * k + e:shift + 2 * k + e + 1],
                                                       in1=tile(n_hi, k, m, a).bitcast(F32), op0=ALU.add, op1=ALU.subtract)
                    ins.then_inc(n_ready, 1)

                for k in range(KD):
                    if k >= 2:
                        dve.wait_ge(n_ready, cnt["n"] + k - 1)
                    for e, (a, m) in parts:
                        ins = dve.scalar_tensor_tensor(out=buf[k % 2][:, a:a + m], in0=tile(x, k, m, a),
                                                       scalar=scale_a[:, 2 * k + e:2 * k + e + 1],
                                                       in1=rstd[:, a:a + m], op0=ALU.mult, op1=ALU.mult)
                    ins.then_inc(t_ready, 1)
                    if k:
                        low(k - 1)
                low(KD - 1)
                cnt["n"] += KD

            def finish(w, i, s):
                n, what = w["base"] + i + 1, w["what"]
                if what.endswith("_up"):
                    if s == 1:
                        m = width(w, 1)
                        dve.wait_ge(unit_done[1], n)
                        dve.wait_ge(pair_free[0], n)
                        if not (isinstance(i, int) and cnt["h"] + i == 0):
                            dve.wait_ge(h_ready, cnt["h"] + i)
                        dve.tensor_tensor(hid_buf[:, 0:m], pair[1][:, 0:m], act_buf[:, 0:m], ALU.mult)\
                           .then_inc(pair_free[1], 1)
                        dve.wait_ge(hhi_ready, cnt["h"] + i + 1)
                        dve.tensor_tensor(tile(h_lo, i, m), hid_buf[:, 0:m], tile(h_hi, i, m).bitcast(F32), ALU.subtract)\
                           .then_inc(h_ready, 1)
                elif what == "in":
                    if s == 1:
                        dve.wait_ge(unit_done[1], n)
                        dst, src = tile(proj, w["arg"] + 2 * i + 1, width(w, 1)), pair[1][:, 0:width(w, 1)]
                        if w["arg"] == T_DQ:
                            ins = dve.tensor_scalar(dst, src, SC_DIFF, None, ALU.mult)
                        else:
                            ins = dve.tensor_copy(dst, src)
                        ins.then_inc(pair_free[1], 1)
                else:
                    dve.wait_ge(unit_done[s], n)
                    for e, (a, m) in enumerate(halves(width(w, s))):
                        xs = tile(x, 2 * i + s, m, a)
                        ins = dve.scalar_tensor_tensor(out=xs, in0=pair[s][:, a:a + m],
                                                       scalar=gate[:, bass.ds((2 * i + s) * 2 + e, 1)], in1=xs,
                                                       op0=ALU.mult, op1=ALU.add)
                    ins.then_inc(pair_free[s], 1)

            def mod_add(w, i):
                b = cnt["batch"] + i
                dve.wait_ge(mod_full, b * 16)
                dve.wait_ge(mod_done, b)
                for k in range(KD):
                    for e in range(2):
                        acc, part = mod_acc[:, e * MOD_W:(e + 1) * MOD_W], mod_w[:, k * MOD_W:(k + 1) * MOD_W]
                        gain = silu_c[:, 2 * k + e:2 * k + e + 1]
                        if k == 0:
                            ins = dve.tensor_scalar(acc, part, gain, None, ALU.mult)
                        else:
                            dve.wait_ge(mod_sum, 2 * KD * (b - 1) + 2 * k + e - 1)
                            ins = dve.scalar_tensor_tensor(out=acc, in0=part, scalar=gain, in1=acc,
                                                           op0=ALU.mult, op1=ALU.add)
                        ins.then_inc(mod_sum, 1)

            def mod_evict(w, i):
                b = cnt["batch"] + i
                dve.wait_ge(mod_done, b + 1)
                for m in range(MOD_T):
                    u = mod_tile(w) + MOD_T * i + m
                    ins = dve.tensor_scalar(mod[:, bass.ds(u * 2, 2)], pair[2][:, 2 * m * P:2 * (m + 1) * P:P],
                                            b_mod[:, bass.ds(u, 1)], None, ALU.add)
                ins.then_inc(mod_out, 1)

            def sweep(q):
                w = SWEEPS[q]
                per = mod_tile(w) is not None
                if not starts_norm(w):
                    split_lo(w, 0, 1)
                if ends_step(w):
                    clear_x()
                if per:
                    mod_add(w, 0)
                finish(w, 0, 0)
                if w["n"] > 1:
                    with dve.Fori(1, w["n"]) as i:
                        split_lo(w, i, 0)
                        finish(w, i - 1, 1)
                        if ends_step(w):
                            add_x(i - 1, 0, width(w, 0))
                        split_lo(w, i, 1)
                        if ends_step(w):
                            add_x(i - 1, 1, width(w, 1))
                        if per:
                            mod_evict(w, i - 1)
                            mod_add(w, i)
                        finish(w, i, 0)
                if q + 1 < len(SWEEPS):
                    split_lo(SWEEPS[q + 1], 0, 0)
                if ends_step(w):
                    add_x(w["n"] - 1, 0, width(w, 0))
                finish(w, w["n"] - 1, 1)
                if per:
                    mod_evict(w, w["n"] - 1)
                    cnt["batch"] += w["n"]
                if w["what"].endswith("_up"):
                    cnt["h"] += FG

            def rotate(L, a, arg, nq_all):
                src = q_rot[:, 0:SEQ] if arg == T_Q else tile(proj, arg, SEQ)
                c, s = (cos_d, sin_d) if T_DQ <= arg < T_DV else (cos_m, sin_m)
                dve.wait_ge(task_done, L * len(TASKS) + a + 1)
                dve.wait_ge(out_dve, L * N_DVE + read_out("d", a))
                dve.tensor_tensor(buf[0][:, 0:SEQ], pair[a % 3][:, 0:SEQ], s[:, :], ALU.mult)
                link(dve.tensor_tensor(buf[1][:, 0:SEQ], src, c[:, :], ALU.mult))
                ins = dve.tensor_tensor(src, buf[0][:, 0:SEQ], buf[1][:, 0:SEQ], ALU.add)
                if arg == T_Q:
                    link(ins)
                    for h in range(HEADS):
                        ins = dve.tensor_copy(mla_q(h, nq_all)[NOPE:, :], q_rot[h * ROPE:(h + 1) * ROPE, 0:nq_all])
                ins.then_inc(out_dve, 1)

            def mixer(L):
                w_last = [w for w in SWEEPS if w["layer"] == L and w["what"] == "in"][-1]
                more = L < DEPTH - 1
                nq_all = TOK if more else SEQ

                def apply(t0, nt, gain, m):
                    wait_rstd()
                    for k in range(nt):
                        ins = dve.scalar_tensor_tensor(out=tile(proj, t0 + k, m), in0=tile(proj, t0 + k, m),
                                                       scalar=gains[:, L * G_LAYER + gain + k:L * G_LAYER + gain + k + 1],
                                                       in1=rstd[:, 0:m], op0=ALU.mult, op1=ALU.mult)
                    ins.then_inc(applied, 1)

                apply(T_KV, 2, G_KVN, TOK)
                for a, (what, arg, who) in enumerate(TASKS):
                    if a == TASKS.index(("rope", T_KR, "d")):
                        apply(T_Q, 3, G_QN, nq_all)
                    if who != "d":
                        continue
                    if what == "qrope":
                        dve.wait_ge(task_done, L * len(TASKS) + a)
                        for h in range(HEADS):
                            ins = dve.tensor_copy(mla_k(h, TOK)[NOPE:, :], tile(proj, T_KR)[NOPE:NOPE + ROPE, :])
                        link(ins)
                        arg = T_Q
                    if arg == T_DQ:
                        dve.wait_ge(tables_full, 16 * 4)
                    if arg == T_KR:
                        dve.wait_ge(mixw_full, 16 * 12 * (L + 1))
                    rotate(L, a, arg, nq_all)

                steps = steps_of(L)
                o_norm = tile(proj, T_DK + 1, SEQ)
                slots = []

                def maxima(kind, nk, n):
                    slots.append(cnt["s"] % 8)
                    for s in (0, 1) if kind == "diff" else (n % 2,):
                        c = cnt["s"] % 8
                        dve.wait_ge(s_ready[s], cnt["sp"][s] + 1)
                        dve.tensor_reduce(neg_max[:, c:c + 1], pair[s][:, 0:nk], AX.X, ALU.max, negate=True)\
                           .then_inc(max_ready, 1)
                        cnt["s"] += 1
                        cnt["sp"][s] += 1

                def normalise(kind, nk, n):
                    e0, c = step_buf(L, n), slots[n]
                    for s in (0, 1) if kind == "diff" else (n % 2,):
                        cnt["ex"][s] += 1
                        dve.wait_ge(exp_done[s], cnt["ex"][s])
                    m = 2 if kind == "diff" else 1
                    link(dve.reciprocal(inv_sum[:, c:c + m], exp_sum[:, c:c + m]))
                    if kind == "diff":
                        dve.tensor_scalar(inv_sum[:, c + 1:c + 2], inv_sum[:, c + 1:c + 2], neg_lam[:, L:L + 1], None,
                                          ALU.mult)
                        link(dve.tensor_scalar(buf[e0][:, 0:nk], buf[e0][:, 0:nk], inv_sum[:, c:c + 1], None, ALU.mult))
                        dve.scalar_tensor_tensor(out=buf[e0][:, 0:nk], in0=buf[e0 + 1][:, 0:nk],
                                                 scalar=inv_sum[:, c + 1:c + 2], in1=buf[e0][:, 0:nk],
                                                 op0=ALU.mult, op1=ALU.add).then_inc(p_ready, 1)
                    else:
                        dve.tensor_scalar(buf[e0][:, 0:nk], buf[e0][:, 0:nk], inv_sum[:, c:c + 1], None, ALU.mult)\
                           .then_inc(p_ready, 1)

                jobs = norm_jobs(L)
                for n in range(len(steps) + 6):
                    if n < len(steps):
                        maxima(steps[n][0][0], steps[n][0][5], n)
                    if 1 <= n <= len(steps):
                        normalise(steps[n - 1][0][0], steps[n - 1][0][5], n - 1)
                    m = n - 2
                    if m - 4 in jobs:
                        _, dh, dq, dn, _, _ = jobs[m - 4]
                        cnt["mhi"] += 1
                        dve.wait_ge(mhi_ready, cnt["mhi"])
                        dve.tensor_tensor(tile(n_lo, M_DIFF + dh, dn, dq), o_norm[:, 0:dn],
                                          tile(n_hi, M_DIFF + dh, dn, dq).bitcast(F32), ALU.subtract).then_inc(mix_ready, 1)
                        cnt["mix"] += 1
                    if m - 2 in jobs:
                        _, dh, dq, dn, _, _ = jobs[m - 2]
                        wait_rstd()
                        if m - 2 > min(jobs):
                            dve.wait_ge(mix_ready, cnt["mix"])
                        dve.scalar_tensor_tensor(out=o_norm[:, 0:dn], in0=tile(proj, T_DQ + dh, dn, dq),
                                                 scalar=sub_gain[:, L:L + 1], in1=rstd[:, 0:dn],
                                                 op0=ALU.mult, op1=ALU.mult).then_inc(otmp_ready, 1)
                    m = n - 3
                    if 0 <= m < len(steps):
                        (kind, h, q0, nq, k0, nk), gi, b = steps[m]
                        if kind == "mla" and h % 2 and b == nq // P - 1:
                            cnt["mla"] += 1
                            dve.wait_ge(mla_hi, cnt["mla"])
                            dve.tensor_tensor(tile(n_lo, M_MLA + h // 2, nq, q0), pair[3][:, 0:nq],
                                              tile(n_hi, M_MLA + h // 2, nq, q0).bitcast(F32), ALU.subtract)\
                               .then_inc(mla_out, 1)
                cnt["mix"] += 2
                for a in range(2):
                    cnt["mhi"] += 1
                    dve.wait_ge(mhi_ready, cnt["mhi"])
                    g = L * G_LAYER + G_POOL + a
                    dve.scalar_tensor_tensor(out=tile(n_lo, M_POOL + a, nq_all), in0=pair[2 + a][:, 0:nq_all],
                                             scalar=gains[:, g:g + 1], in1=tile(n_hi, M_POOL + a, nq_all).bitcast(F32),
                                             op0=ALU.mult, op1=ALU.subtract).then_inc(mix_ready, 1)

            for q, w in enumerate(SWEEPS):
                L = w["layer"]
                if starts_norm(w):
                    chunk, gain = {"ffn1_up": (0, G_FFN1), "in": (3, G_MIX), "ffn2_up": (6, G_FFN2)}[w["what"]]
                    norm_x(w, norm_width(w), L, L * G_LAYER + gain, mod_col(L, chunk))
                if w["what"] == "out":
                    mixer(L)
                if w["arg"] == 0 and w["what"] in ("ffn1_down", "ffn2_down", "out"):
                    c = mod_col(L, {"ffn1_down": 2, "out": 5, "ffn2_down": 8}[w["what"]])
                    dve.wait_ge(mod_out, cnt["batch"])
                    link(dve.tensor_scalar(gate[:, :], mod[:, c:c + 16], 1.0 if w["what"] == "out" else 0.5, None, ALU.mult))
                sweep(q)
            wait_rstd()
            for k in range(KD):
                dve.scalar_tensor_tensor(out=tile(x, k, SEQ), in0=tile(x, k, SEQ), scalar=gains[:, G_FINAL + k:G_FINAL + k + 1],
                                         in1=rstd[:, 0:SEQ], op0=ALU.mult, op1=ALU.mult).then_inc(n_ready, 1)

        @block.gpsimd
        def _(pool):
            links = 0

            def link(ins):
                nonlocal links
                links += 1
                ins.then_inc(pool_chain, 1)
                pool.wait_ge(pool_chain, links)

            def window_sums(length, view, g):
                src, dst = pool_a, pool_b
                for level in range(1, 2 * g + 3):
                    parts = slice(64, P) if level == 2 * g + 2 else slice(0, P)
                    lo, hi = 1 << (level - 1), length - (0, 0, 1, 3, 8)[level]
                    back, ahead = (1, 0) if level == 1 else (1 << (level - 2),) * 2
                    link(pool.tensor_tensor(view(dst, parts, lo, hi), view(src, parts, lo - back, hi - back),
                                            view(src, parts, lo + ahead, hi + ahead), ALU.add))
                    src, dst = dst, src

            both = ((slice(0, 64), pool_b), (slice(64, P), pool_a))
            wide = GRID_W + 2 * PAD

            def grid_rows(tensor, parts, lo, hi):
                return tensor[parts, lo * GRID_W:hi * GRID_W]

            def grid_cols(tensor, parts, lo, hi):
                return tensor[parts, 0:ROWS * wide].rearrange("p (r c) -> p r c", r=ROWS)[:, :, lo:hi]

            def line(tensor, parts, lo, hi):
                return tensor[parts, lo:hi]

            def as_grid(ap):
                return ap.rearrange("p (r c) -> p r c", r=ROWS)

            def counts(parts, g, at, n):
                return pool_inv[parts, g * N_COUNTS + at:g * N_COUNTS + at + n]

            for L in range(DEPTH):
                w_last = [w for w in SWEEPS if w["layer"] == L and w["what"] == "in"][-1]
                for s in range(2):
                    pool.wait_ge(unit_done[s], w_last["base"] + w_last["n"])
                    pool.wait_ge(pair_free[s], w_last["base"] + w_last["n"])
                pool.memset(pool_w[:, :], 0.0).then_inc(poolw_zero, 1)
                pool.wait_ge(counts_full, 16 * (L + 1))
                for g in range(2):
                    link(pool.memset(pool_a[:, :], 0.0))
                    link(pool.tensor_copy(grid_rows(pool_a, slice(0, P), PAD, PAD + ROWS), tile(proj, g, SEQ)))
                    window_sums(ROWS + 2 * PAD, grid_rows, g)
                    for parts, src in both:
                        link(pool.tensor_tensor(as_grid(pool_c[parts, :]), as_grid(grid_rows(src, parts, PAD, PAD + ROWS)),
                                                counts(parts, g, 0, ROWS).unsqueeze(2).broadcast_to([64, ROWS, GRID_W]),
                                                ALU.mult))
                    link(pool.memset(pool_a[:, 0:ROWS * wide], 0.0))
                    link(pool.tensor_copy(grid_cols(pool_a, slice(0, P), PAD, PAD + GRID_W), as_grid(pool_c[:, :])))
                    window_sums(wide, grid_cols, g)
                    for parts, src in both:
                        link(pool.tensor_tensor(as_grid(pool_c[parts, :]), grid_cols(src, parts, PAD, PAD + GRID_W),
                                                counts(parts, g, ROWS, GRID_W).unsqueeze(1).broadcast_to([64, ROWS, GRID_W]),
                                                ALU.mult))
                    ins = pool.tensor_tensor(tile(proj, g, SEQ), pool_c[:, :], tile(proj, g, SEQ), ALU.subtract)
                    if L < DEPTH - 1:
                        link(ins)
                        link(pool.memset(pool_a[:, 0:CTX + 2 * PAD], 0.0))
                        link(pool.tensor_copy(pool_a[:, PAD:PAD + CTX], tile(proj, g, CTX, SEQ)))
                        window_sums(CTX + 2 * PAD, line, g)
                        for parts, src in both:
                            link(pool.tensor_tensor(pool_c[parts, 0:CTX], src[parts, PAD:PAD + CTX],
                                                    counts(parts, g, ROWS + GRID_W, CTX), ALU.mult))
                        ins = pool.tensor_tensor(tile(proj, g, CTX, SEQ), pool_c[:, 0:CTX], tile(proj, g, CTX, SEQ),
                                                 ALU.subtract)
                    ins.then_inc(pool_ready, 1)
                    pool.wait_ge(pool_ready, 2 * L + g + 1)


_INS = ["x", "c", "ctx", "c_ctx", "w_mod", "b_mod", "ffn1_norm", "ffn1_w1", "ffn1_w3", "ffn1_w2", "mix_norm", "w_in",
        "w_out", "pool_w", "pool_scale", "mla_q_norm", "mla_w_uq", "mla_kv_norm", "mla_w_ukv", "diff_lambda",
        "diff_subln", "ffn2_norm", "ffn2_w1", "ffn2_w3", "ffn2_w2", "final_norm"]


def rope_tables(dim):
    n_axis = dim // 4
    at = np.arange(SEQ)
    inv = (ROPE_BASE ** (-np.arange(n_axis) / n_axis)).astype(np.float32)
    ang = np.concatenate([(at // GRID_W)[:, None].astype(np.float32) * inv,
                          (at % GRID_W)[:, None].astype(np.float32) * inv], axis=-1)
    p = np.arange(P)
    cos, sin = np.cos(ang)[:, p % (dim // 2)].T, np.sin(ang)[:, p % (dim // 2)].T
    sign = np.where(p % dim < dim // 2, -1.0, 1.0)[:, None]
    swap = np.zeros((P, P), np.float32)
    swap[p ^ (dim // 2), p] = 1.0
    return cos.astype(np.float32), (sin * sign).astype(np.float32), swap


def window_counts():
    def inverse(n, k):
        i = np.arange(n)
        return 1.0 / (np.clip(i + k - k // 2, 0, n) - np.clip(i - k // 2, 0, n))

    inv = np.zeros((P, 2, N_COUNTS), np.float32)
    for g, k in enumerate(WINDOWS):
        parts = slice(64 * (g % 2), 64 * (g % 2) + 64)
        inv[parts, g // 2] = np.concatenate([inverse(ROWS, k), inverse(GRID_W, k), inverse(CTX, k)])
    return inv.reshape(P, 2 * N_COUNTS)


def kernel(**inputs):
    import concourse.bacc as bacc
    from concourse.bass_utils import run_bass_kernel_spmd

    cos_d, sin_d, perm_d = rope_tables(DDIM)
    cos_m, sin_m, perm_m = rope_tables(ROPE)
    arrays = {f"in_{n}": np.ascontiguousarray(inputs[n]) for n in _INS}
    arrays.update(k_ident=np.eye(P, dtype=np.float32), k_perm_d=perm_d, k_perm_m=perm_m, k_cos_d=cos_d, k_sin_d=sin_d,
                  k_cos_m=cos_m, k_sin_m=sin_m, k_pool_inv=window_counts())
    nc = bacc.Bacc("TRN2", target_bir_lowering=False, num_devices=1)
    tensors = {n.removeprefix("in_"): nc.dram_tensor(n, a.shape, mybir.dt.from_np(a.dtype), kind="ExternalInput").ap()
               for n, a in arrays.items()}
    out = nc.dram_tensor("out", (1, SEQ, D), F32, kind="ExternalOutput").ap()
    build(nc, tensors, out)
    result = run_bass_kernel_spmd(nc, [arrays], core_ids=[0])
    return result.results[0]["out"]
```
